# Optimizing a Trainium2 kernel written in Bass

```python
import math
import jax, jax.numpy as jnp
from jax import lax
import numpy as np

D_MODEL = 1024
BATCH = 1
SEQ = 128
DEPTH = 2
DEC_BATCH = 1
DEC_SEQ = 512
PAST_LEN = 128

GRID_W = 64
HEAD_DIM = 64
N_HEADS = 8
N_KV_HEADS = 2
GROUP = N_HEADS // N_KV_HEADS
ATTN_W = N_HEADS * HEAD_DIM
KV_W = N_KV_HEADS * HEAD_DIM
WINDOW = 128
BLOCK = 128
HY_W = 512
FILT_EMB = 33
FILT_BANDS = (FILT_EMB - 1) // 2
FILT_HIDDEN = 64
D_FF = 2816
CONV_W = 3
ROPE_BASE = 10000.0
LN_EPS = 1e-5
DEEPNORM_ALPHA = (2 * DEPTH) ** 0.25
DEEPNORM_BETA = (8 * DEPTH) ** -0.25
IN_COLS = ATTN_W + 2 * KV_W + 3 * HY_W + 2 * D_MODEL
SPLITS = [ATTN_W, ATTN_W + KV_W, ATTN_W + 2 * KV_W, ATTN_W + 2 * KV_W + 3 * HY_W,
          ATTN_W + 2 * KV_W + 3 * HY_W + D_MODEL]

kernel_name = 'hybrid_dit_swa_hyena_deepnorm_step'

def layer_norm(x, g, b):
    xf = x.astype(jnp.float32)
    mu = jnp.mean(xf, axis=-1, keepdims=True)
    var = jnp.mean(jnp.square(xf - mu), axis=-1, keepdims=True)
    y = (xf - mu) * lax.rsqrt(var + LN_EPS) * g.astype(jnp.float32) + b.astype(jnp.float32)
    return y.astype(x.dtype)

def centred_dwconv(x, w, b):
    L = x.shape[1]
    xp = jnp.pad(x, ((0, 0), (1, 1), (0, 0)))
    return xp[:, :L] * w[0] + xp[:, 1:L + 1] * w[1] + xp[:, 2:] * w[2] + b

def axial_rope(x):
    L = x.shape[1]
    rows = L // GRID_W
    r, col = jnp.meshgrid(jnp.arange(rows), jnp.arange(GRID_W), indexing='ij')
    pos = jnp.stack([r.reshape(-1), col.reshape(-1)], axis=-1).astype(jnp.float32)
    half = HEAD_DIM // 2
    inv_freq = 1.0 / (ROPE_BASE ** (jnp.arange(0, half, 2, dtype=jnp.float32) / half))
    ang = pos[:, :, None] * inv_freq
    ang = jnp.stack([ang, ang], axis=-2).reshape(L, HEAD_DIM)
    cos = jnp.cos(ang)[None, :, None, :]
    sin = jnp.sin(ang)[None, :, None, :]
    xf = x.astype(jnp.float32)
    xa = xf.reshape(x.shape[:-1] + (2, 2, HEAD_DIM // 4))
    rot = jnp.stack([-xa[..., 1, :], xa[..., 0, :]], axis=-2).reshape(x.shape)
    return (xf * cos + rot * sin).astype(x.dtype)

def softmax_with_sink(logits, sink):
    s = sink[None, :, :, None, None]
    m = jnp.maximum(jnp.max(logits, axis=-1, keepdims=True), s)
    e = jnp.exp(logits - m)
    return e / (jnp.sum(e, axis=-1, keepdims=True) + jnp.exp(s - m))

def context_attention(q, k, v, sink):
    B, Lc = q.shape[:2]
    nb = Lc // BLOCK
    qb = q.reshape(B, nb, BLOCK, N_KV_HEADS, GROUP, HEAD_DIM).transpose(1, 0, 2, 3, 4, 5)
    s_sink = sink.reshape(N_KV_HEADS, GROUP).astype(jnp.float32)
    kf = k.astype(jnp.float32)
    vf = v.astype(jnp.float32)
    scale = HEAD_DIM ** -0.5

    def one_block(qblk):
        logits = jnp.einsum('bqkgd,bskd->bkgqs', qblk.astype(jnp.float32), kf) * scale
        p = softmax_with_sink(logits, s_sink)
        return jnp.einsum('bkgqs,bskd->bqkgd', p, vf)

    out = lax.map(one_block, qb)
    return out.transpose(1, 0, 2, 3, 4, 5).reshape(B, Lc, ATTN_W).astype(q.dtype)

def latent_attention(q, k, v, k_ctx, v_ctx, sink):
    B, L = q.shape[:2]
    Lc = k_ctx.shape[1]
    nb = L // BLOCK
    span = BLOCK + 2 * WINDOW
    qb = q.reshape(B, nb, BLOCK, N_KV_HEADS, GROUP, HEAD_DIM).transpose(1, 0, 2, 3, 4, 5)
    kp = jnp.pad(k.astype(jnp.float32), ((0, 0), (WINDOW, WINDOW), (0, 0), (0, 0)))
    vp = jnp.pad(v.astype(jnp.float32), ((0, 0), (WINDOW, WINDOW), (0, 0), (0, 0)))
    kc = k_ctx.astype(jnp.float32)
    vc = v_ctx.astype(jnp.float32)
    s_sink = sink.reshape(N_KV_HEADS, GROUP).astype(jnp.float32)
    scale = HEAD_DIM ** -0.5

    def one_block(args):
        bi, qblk = args
        start = bi * BLOCK
        kb = lax.dynamic_slice_in_dim(kp, start, span, axis=1)
        vb = lax.dynamic_slice_in_dim(vp, start, span, axis=1)
        qpos = start + jnp.arange(BLOCK)
        kpos = start - WINDOW + jnp.arange(span)
        mask = (jnp.abs(qpos[:, None] - kpos[None, :]) <= WINDOW) & (kpos >= 0)[None, :] & (kpos < L)[None, :]
        qf = qblk.astype(jnp.float32)
        l_ctx = jnp.einsum('bqkgd,bskd->bkgqs', qf, kc) * scale
        l_band = jnp.einsum('bqkgd,bskd->bkgqs', qf, kb) * scale
        l_band = jnp.where(mask[None, None, None], l_band, -jnp.inf)
        p = softmax_with_sink(jnp.concatenate([l_ctx, l_band], axis=-1), s_sink)
        return (jnp.einsum('bkgqs,bskd->bqkgd', p[..., :Lc], vc)
                + jnp.einsum('bkgqs,bskd->bqkgd', p[..., Lc:], vb))

    out = lax.map(one_block, (jnp.arange(nb), qb))
    return out.transpose(1, 0, 2, 3, 4, 5).reshape(B, L, ATTN_W).astype(q.dtype)

def hyena_decay_rates():
    target = 1e-2
    max_decay = math.log(target) / 0.3
    min_decay = math.log(target) / 1.5
    return jnp.abs(jnp.linspace(min_decay, max_decay, HY_W, dtype=jnp.float32))

def hyena_filters(L, lp):
    t = jnp.linspace(0.0, 1.0, L, dtype=jnp.float32)[:, None]
    w = 2.0 * math.pi * jnp.arange(L, dtype=jnp.float32) / L
    f = jnp.linspace(1e-4, FILT_BANDS - 1, FILT_BANDS, dtype=jnp.float32)
    zr = w[:, None] * f[None, :]
    feats = jnp.concatenate([t, jnp.cos(zr), -jnp.sin(zr)], axis=-1)
    h = jnp.sin(lp['filt_freq1'].astype(jnp.float32) * (feats @ lp['filt_w1'].astype(jnp.float32) + lp['filt_b1'].astype(jnp.float32)))
    h = jnp.sin(lp['filt_freq2'].astype(jnp.float32) * (h @ lp['filt_w2'].astype(jnp.float32) + lp['filt_b2'].astype(jnp.float32)))
    h = (h @ lp['filt_w3'].astype(jnp.float32)).reshape(L, 2, HY_W)
    window = jnp.exp(-t * hyena_decay_rates()[None, :])
    return h * window[:, None, :]

def bidir_long_conv(u, h, bias):
    L, C = u.shape[1], u.shape[2]
    g = jnp.concatenate([h[:, 0], jnp.zeros((1, C), jnp.float32), h[:0:-1, 1]], axis=0)
    U = jnp.fft.rfft(u, n=2 * L, axis=1)
    G = jnp.fft.rfft(g, n=2 * L, axis=0)
    y = jnp.fft.irfft(U * G[None], n=2 * L, axis=1)[:, :L]
    return y + u * bias

def hyena_branch(z, lp):
    z = centred_dwconv(z, lp['hy_conv_w'], lp['hy_conv_b'])
    x0, x1, u = jnp.split(z, 3, axis=-1)
    h = hyena_filters(z.shape[1], lp)
    y = bidir_long_conv((x1 * u).astype(jnp.float32), h, lp['hy_bias'].astype(jnp.float32))
    return x0 * y.astype(z.dtype)

def conv_ffn(h, lp):
    gate, val = jnp.split(h @ lp['w_up'], 2, axis=-1)
    gate = centred_dwconv(gate, lp['ffn_conv_w'], lp['ffn_conv_b'])
    return (jax.nn.gelu(gate, approximate=False) * val) @ lp['w_down']

def trunk_layer(x, cond, lp, ctx_k=None, ctx_v=None):
    mod = jax.nn.silu(cond) @ lp['w_ada'] + lp['b_ada']
    sh1, sc1, g1, sh2, sc2, g2 = jnp.split(mod[:, None, :], 6, axis=-1)
    B, L, _ = x.shape
    h = x * (1.0 + sc1) + sh1
    q, k, v, z_hy, gate_a, gate_b = jnp.split(h @ lp['w_in'], SPLITS, axis=-1)
    q = q.reshape(B, L, N_HEADS, HEAD_DIM)
    k = k.reshape(B, L, N_KV_HEADS, HEAD_DIM)
    v = v.reshape(B, L, N_KV_HEADS, HEAD_DIM)
    if ctx_k is None:
        attn = context_attention(q, k, v, lp['attn_sink'])
    else:
        attn = latent_attention(axial_rope(q), axial_rope(k), v, ctx_k, ctx_v, lp['attn_sink'])
    hy = hyena_branch(z_hy, lp)
    merged = jax.nn.sigmoid(gate_a) * (attn @ lp['w_pa']) + jax.nn.sigmoid(gate_b) * (hy @ lp['w_pb'])
    x = layer_norm(DEEPNORM_ALPHA * x + g1 * (merged @ lp['w_out']), lp['ln1_g'], lp['ln1_b'])
    ffn = conv_ffn(x * (1.0 + sc2) + sh2, lp)
    x = layer_norm(DEEPNORM_ALPHA * x + g2 * ffn, lp['ln2_g'], lp['ln2_b'])
    return x, k, v

def setup_inputs(seed: int = 0) -> dict:
    key = jax.random.key(seed)
    ks = jax.random.split(key, 32)

    def nrm(k, shape, scale):
        return jax.random.normal(k, shape, jnp.float32) * scale

    return {
        'x_prompt': nrm(ks[0], (BATCH, SEQ, D_MODEL), 1.0),
        'x_sample': nrm(ks[1], (DEC_BATCH, DEC_SEQ, D_MODEL), 1.0),
        'cache_k': nrm(ks[2], (DEC_BATCH, DEPTH, PAST_LEN, N_KV_HEADS, HEAD_DIM), 1.0),
        'cache_v': nrm(ks[3], (DEC_BATCH, DEPTH, PAST_LEN, N_KV_HEADS, HEAD_DIM), 1.0),
        'c': nrm(ks[4], (DEC_BATCH, D_MODEL), 1.0),
        'c_ctx': nrm(ks[5], (D_MODEL,), 1.0),
        'w_ada': nrm(ks[6], (DEPTH, D_MODEL, 6 * D_MODEL), D_MODEL ** -0.5),
        'b_ada': nrm(ks[7], (DEPTH, 6 * D_MODEL), 0.01),
        'w_in': nrm(ks[8], (DEPTH, D_MODEL, IN_COLS), D_MODEL ** -0.5),
        'attn_sink': nrm(ks[9], (DEPTH, N_HEADS), 1.0),
        'hy_conv_w': nrm(ks[10], (DEPTH, CONV_W, 3 * HY_W), CONV_W ** -0.5),
        'hy_conv_b': nrm(ks[11], (DEPTH, 3 * HY_W), 0.01),
        'filt_w1': nrm(ks[12], (DEPTH, FILT_EMB, FILT_HIDDEN), FILT_EMB ** -0.5),
        'filt_b1': nrm(ks[13], (DEPTH, FILT_HIDDEN), 0.01),
        'filt_freq1': 1.0 + nrm(ks[14], (DEPTH, FILT_HIDDEN), 0.01),
        'filt_w2': nrm(ks[15], (DEPTH, FILT_HIDDEN, FILT_HIDDEN), FILT_HIDDEN ** -0.5),
        'filt_b2': nrm(ks[16], (DEPTH, FILT_HIDDEN), 0.01),
        'filt_freq2': 1.0 + nrm(ks[17], (DEPTH, FILT_HIDDEN), 0.01),
        'filt_w3': nrm(ks[18], (DEPTH, FILT_HIDDEN, 2 * HY_W), FILT_HIDDEN ** -0.5),
        'hy_bias': nrm(ks[19], (DEPTH, HY_W), 1.0),
        'w_pa': nrm(ks[20], (DEPTH, ATTN_W, D_MODEL), ATTN_W ** -0.5),
        'w_pb': nrm(ks[21], (DEPTH, HY_W, D_MODEL), HY_W ** -0.5),
        'w_out': nrm(ks[22], (DEPTH, D_MODEL, D_MODEL), D_MODEL ** -0.5 * DEEPNORM_BETA),
        'ln1_g': 1.0 + nrm(ks[23], (DEPTH, D_MODEL), 0.01),
        'ln1_b': nrm(ks[24], (DEPTH, D_MODEL), 0.01),
        'w_up': nrm(ks[25], (DEPTH, D_MODEL, 2 * D_FF), D_MODEL ** -0.5),
        'ffn_conv_w': nrm(ks[26], (DEPTH, CONV_W, D_FF), CONV_W ** -0.5),
        'ffn_conv_b': nrm(ks[27], (DEPTH, D_FF), 0.01),
        'w_down': nrm(ks[28], (DEPTH, D_FF, D_MODEL), D_FF ** -0.5 * DEEPNORM_BETA),
        'ln2_g': 1.0 + nrm(ks[29], (DEPTH, D_MODEL), 0.01),
        'ln2_b': nrm(ks[30], (DEPTH, D_MODEL), 0.01),
    }

def reference(x_prompt, x_sample, cache_k, cache_v, c, c_ctx, w_ada, b_ada, w_in, attn_sink,
              hy_conv_w, hy_conv_b, filt_w1, filt_b1, filt_freq1, filt_w2, filt_b2, filt_freq2,
              filt_w3, hy_bias, w_pa, w_pb, w_out, ln1_g, ln1_b, w_up, ffn_conv_w, ffn_conv_b,
              w_down, ln2_g, ln2_b):
    y_prompt = x_prompt
    y_sample = x_sample
    keys, values = [], []
    for l in range(DEPTH):
        lp = {
            'w_ada': w_ada[l], 'b_ada': b_ada[l], 'w_in': w_in[l], 'attn_sink': attn_sink[l],
            'hy_conv_w': hy_conv_w[l], 'hy_conv_b': hy_conv_b[l],
            'filt_w1': filt_w1[l], 'filt_b1': filt_b1[l], 'filt_freq1': filt_freq1[l],
            'filt_w2': filt_w2[l], 'filt_b2': filt_b2[l], 'filt_freq2': filt_freq2[l],
            'filt_w3': filt_w3[l], 'hy_bias': hy_bias[l],
            'w_pa': w_pa[l], 'w_pb': w_pb[l], 'w_out': w_out[l], 'ln1_g': ln1_g[l], 'ln1_b': ln1_b[l],
            'w_up': w_up[l], 'ffn_conv_w': ffn_conv_w[l], 'ffn_conv_b': ffn_conv_b[l],
            'w_down': w_down[l], 'ln2_g': ln2_g[l], 'ln2_b': ln2_b[l],
        }
        y_prompt, k_l, v_l = trunk_layer(y_prompt, c_ctx[None, :], lp)
        keys.append(k_l)
        values.append(v_l)
        y_sample, _, _ = trunk_layer(y_sample, c, lp, cache_k[:, l], cache_v[:, l])
    new_cache_k = jnp.stack(keys, axis=1)
    new_cache_v = jnp.stack(values, axis=1)
    return (y_prompt, y_sample, new_cache_k, new_cache_v)


_drawn_inputs = setup_inputs


def setup_inputs(seed=0):
    import zlib

    import numpy as np

    out = dict(_drawn_inputs(seed))
    spreads = {}
    factors = {'cache_k': 8.0,
     'cache_v': 7.622,
     'attn_sink': 8.0,
     'filt_freq1': 6.267,
     'filt_freq2': 3.875,
     'ln1_g': 3.356,
     'ln1_b': 2.882,
     'ffn_conv_b': 8.0,
     'ln2_g': 3.355,
     'ln2_b': 8.323}
    for name, (base, spread) in spreads.items():
        noise = np.random.default_rng([zlib.crc32(name.encode()), seed]).standard_normal(out[name].shape)
        drawn = base * np.exp(spread * noise) if base else spread * noise
        out[name] = __import__('jax').numpy.asarray(drawn.astype(out[name].dtype))
    for name, factor in factors.items():
        out[name] = (out[name] * factor).astype(out[name].dtype)
    return out
```

```python
import math
from contextlib import ExitStack

import numpy as np
import concourse.bass as bass
from concourse import mybir

F32 = mybir.dt.float32
F32R = mybir.dt.float32r
BF16 = mybir.dt.bfloat16
ACT = mybir.ActivationFunctionType
ALU = mybir.AluOpType

P = 128
D_MODEL, DEPTH = 1024, 2
SEQ, DEC_SEQ, PAST = 128, 512, 128
HD, NH, NKV = 64, 8, 2
HY_W, D_FF = 512, 2816
ALPHA = (2 * DEPTH) ** 0.25
LN_EPS = 1e-5
KD = D_MODEL // P
NB = (SEQ + DEC_SEQ) // P
ROW = SEQ + DEC_SEQ + 4
HALF = ROW // 2
C0, L0 = 1, SEQ + 3
CTX, LAT = slice(C0, C0 + SEQ), slice(L0, L0 + DEC_SEQ)
NFF = D_FF // P
FH = NFF // 2
NHY = HY_W // P

CHUNK = 2048
ADA_STEPS = 6 * D_MODEL // 256
ADA_FIRST = 2 * D_MODEL // 256
ADA_GROUP = D_MODEL // 256
DOWN_W = FH * P
F0_BLOCKS, F1_BLOCKS = 14, 16
GEMM = ([("q", 0), ("q", 1), ("k", 0), ("v", 0)] + [("z", i) for i in range(6)]
        + [("F", 0), ("F", 1), ("F", 0), ("I", 0), ("F", 1), ("I", 1)]
        + [x for m in range(KD) for x in (("gate", m), ("proj", m))]
        + [("out", i) for i in range(4)]
        + [("up", j) for j in range(FH)] + [("down", m) for m in range(KD)]
        + [("up", FH + j) for j in range(FH)] + [("down", KD + m) for m in range(KD)])
NG = len(GEMM)
WIDTH = {"q": 2048, "k": 1024, "v": 1024, "z": 2048, "gate": 2048, "proj": 1024, "out": 2048,
         "up": 2048, "down": DOWN_W}
WG = [g for g in range(NG) if GEMM[g][0] not in "FI"]


def width(g):
    kind, i = GEMM[g]
    if kind == "F":
        return (F0_BLOCKS, F1_BLOCKS)[i] * P
    return CHUNK if kind == "I" else WIDTH[kind]


def stream():
    order = [(0, "ada", s) for s in range(ADA_FIRST)]
    gf = at_g("F", 0)
    for layer in range(DEPTH):
        for g in range(NG):
            order.append((layer, "g", g))
            if layer == 0 and gf - 3 <= g <= gf:
                first = ADA_FIRST + ADA_GROUP * (g - gf + 3)
                order += [(layer, "ada", s) for s in range(first, first + ADA_GROUP)]
            if layer + 1 < DEPTH and g - 1 in ADA_FFN:
                order.append((layer + 1, "ada", ADA_FFN[g - 1]))
    return order


def at_g(kind, i=0, nth=0):
    return [g for g in range(NG) if GEMM[g] == (kind, i)][nth]


ADA_FFN = {g: n for n, g in enumerate([g for g in range(at_g("up"), NG) if GEMM[g][0] == "up" or GEMM[g][1] < 2])}
assert len(ADA_FFN) == ADA_STEPS

PAR = {}
NPAR = 0
for _name, _n in (("b_ada", 48), ("hy_w", 36), ("hy_b", 12), ("hy_bias", 4), ("ln1_g", 8),
                  ("ln1_b", 8), ("ln2_g", 8), ("ln2_b", 8), ("ff_w", 66), ("ff_b", 22),
                  ("sink", 8), ("cache_k", 128), ("cache_v", 128)):
    PAR[_name] = NPAR
    NPAR += _n

FEAT = 33
NT = 2 * (SEQ + DEC_SEQ)
PAIRS = 5
SH1, SC1, G1, SH2, SC2, G2 = (8 * _i for _i in range(6))

KEYS = [[("own", 0, 1)], [("lat", 0, 2), ("ctx", 0, 1)], [("ctx", 0, 1), ("lat", 0, 3)],
        [("ctx", 0, 1), ("lat", 1, 3)], [("ctx", 0, 1), ("lat", 2, 2)]]
MASK_AT = [0, 2, 0, 0, 0]
TWO_PI_PARTS = (6.28125, 0.0019350051879882812, 3.0199159819120541e-07)
MAGIC = 12582912.0
KV_SPACE = 3 * HY_W

EVENTS = dict(
    params_in=16, trig_in=16, w3_in=16, win_in=16 * 3, mod_done=6, w_hi=NG, w_split=NG,
    h_src=3 * KD, h_hi=3 * KD, h_ready=3 * KD, x_scaled=2 * KD,
    qkv_mm=6, qkv_out=6, rot_mm=5, rot_out=5, vt_mm=2, vt_out=4,
    z_mm=12, z_raw=12, z_acc=12, z_out=12, xu_ready=4,
    qk_mm=40, qk_out=40, soft_m=5, exp_out=40,
    pt_mm=40, pt_act=20, pt_dve=20, pv_mm=40, osb_out=5, ot_mm=5, at_hi=5, at_lo=5,
    filt_mm=10, filt_out=10, gs_src=10, gs_hi=10, gs_ready=10, gsp_mm=10, gsp_out=10,
    ut_mm=5, ut_out=5, us_src=9, us_hi=9, us_ready=9, usp_mm=10, usp_out=10,
    y_src=10, y_hi=10, y_ready=10, cinv_mm=1, cinv_out=1, linv_mm=4, hy_src=4, hy_hi=4, hy_ready=4,
    gate_mm=16, gate_out=16, proj_mm=16, proj_out=16, m_src=8, m_hi=8, m_ready=8,
    out_mm=8, out_out=8, up_mm=44, up_raw=22, up_acc=22, up_taps=22, up_gelu=22, up_out=22,
    act_hi=22, act_ready=22, down_mm=16, down_out=16, sq_out=16, sum1_out=16, sum2_out=16,
    stat_mm=2, ln_var=2, ln_sqrt=2, diag_out=2, bc_mm=2, ln_norm=16, ln_x=16,
    pads_h=3, pads_at=1, kv_dma=32, dve_order=1, act_order=1, pool_order=1,
)
CREDIT = dict(w_split=2, down_mm=2, ln_x=1, m_ready=1, h_ready=1)


class Counts:

    def __init__(self, order):
        self.order = order
        self.layer, self.n, self.before = 0, {}, 0

    def start(self, layer):
        self.before += self.n.get(self.order, 0)
        self.layer, self.n = layer, {}

    def raised(self, event):
        self.n[event] = self.n.get(event, 0) + 1
        return 1

    def due(self, event, n):
        return self.layer * EVENTS[event] + CREDIT.get(event, 0) + n

    def now(self, event):
        if event == self.order:
            return self.before + self.n[event]
        return self.due(event, self.n[event])

    def end(self):
        for e, n in self.n.items():
            assert e == self.order or n == EVENTS[e], (e, n, EVENTS[e])


def _program(nc, A):
    st = ExitStack()
    sem = {n: st.enter_context(nc.semaphore(n)) for n in EVENTS}
    for n in ("raw0", "raw1", "ada_mm", "row_first", "row_act", "row_dve", "col_mm", "ada_t", "cond_rows_in", "cond_rows", "cond_in", "x_in", "consts_in", "x_zero", "cond_ready", "x_tr", "x_row", "mlp_mm", "mlp_arg", "mlp_sin",
              "mlp_order", "mask_done", "y_mm", "y_out", "y_dma"):
        sem[n] = st.enter_context(nc.semaphore(n))

    def sb(name, shape, dt=F32, where=st):
        return where.enter_context(nc.sbuf_tensor(name, shape, dt))

    x = sb("x", [P, KD, ROW])
    raw = [sb(f"w_raw{i}", [P, CHUNK]) for i in range(2)]
    whi = [sb(f"w_hi{i}", [P, CHUNK], F32R) for i in range(2)]
    wlo = [sb(f"w_lo{i}", [P, CHUNK], F32R) for i in range(2)]
    par = sb("par", [P, -(-NPAR // 16) * 16])
    ident = sb("ident", [P, P])
    rot = sb("rot", [P, P])
    ones = sb("ones", [P, P])
    mask = sb("mask", [P, 5 * P], BF16)
    h2T = sb("h2T", [P, NT])
    cs = sb("cs", [P, KD, 2])
    mod = sb("mod", [P, 48, 2])
    small = sb("small", [P, 96])

    with ExitStack() as s:
        trig = sb("trig", [P, 2, DEC_SEQ], F32, s)
    with ExitStack() as s:
        prod = sb("prod", [P, 2, HY_W], F32, s)
    with ExitStack() as s:
        hsrc = sb("h_src_rows", [P, 2, ROW], F32, s)
    with ExitStack() as s:
        sb("trig_space", [P, 2 * DEC_SEQ], F32, s)
        rows = sb("mod_rows", [P, 2, P], F32, s)
    gates = sb("gates", [P, 2, ROW])
    with ExitStack() as s:
        rows0 = sb("mod_rows_first", [P, 4 * ADA_GROUP, P], F32, s)
        xin = sb("x_in", [P, NB, D_MODEL], F32, s)
        feat = sb("feat", [FEAT, NT], F32, s)
        mask_in = sb("mask_in", [P, 5 * P], F32, s)
        w1 = sb("w1", [FEAT, P], F32, s)
        w2 = sb("w2", [P, P], F32, s)
        mlpv = sb("mlp_vec", [P, 4], F32, s)
        h1T = sb("h1T", [P, NT], F32, s)
    with ExitStack() as s:
        yout = sb("y_rows", [P, 2, D_MODEL], F32, s)
    with ExitStack() as s:
        vhi = sb("v_hi", [P, 10, HY_W], F32R, s)
        vlo = sb("v_lo", [P, 10, HY_W], F32R, s)
    hhi = sb("h_hi", [P, KD, ROW], F32R)
    hlo = sb("h_lo", [P, KD, ROW], F32R)
    with ExitStack() as s:
        with ExitStack() as s2:
            q = sb("q", [P, 4, ROW], F32, s2)
        ath = sb("attn_hi", [P, 4, ROW], F32R, s)
        with ExitStack() as s2:
            k = sb("k", [P, 1, ROW], F32, s2)
            vtok = sb("v_tok", [P, NB, P], F32, s2)
        with ExitStack() as s2:
            w3 = sb("w3", [P, 2 * HY_W], F32, s2)
            dreg = sb("d_block", [P, HY_W], F32, s2)
        with ExitStack() as s2:
            us = sb("u_spec", [P, 2, HY_W], F32, s2)
        sb("k_v_space", [P, KV_SPACE], F32, s)
        atl = sb("attn_lo", [P, 4, ROW], F32R, s)
        x0c = sb("x0c", [P, NHY, ROW], F32, s)
        xu = sb("xu", [P, NHY, ROW], F32, s)
        with ExitStack() as s2:
            sc = sb("scores", [P, NH, 4 * P], F32, s2)
            pt = sb("p_t", [P, 2, 4 * P], F32, s2)
            osb = sb("o_sb", [P, 4 * P], F32, s2)
            kcT = sb("kcT", [P, P], F32, s2)
            kout = sb("k_out", [P, P], F32, s2)
            zt = sb("z_rows", [P, 2, ROW], F32, s2)
            ca = sb("z_acc", [P, 2, ROW], F32, s2)
        with ExitStack() as s2:
            hyh = sb("hy_hi", [P, NHY, ROW], F32R, s2)
            hyl = sb("hy_lo", [P, NHY, ROW], F32R, s2)
        with ExitStack() as s2:
            gsp = sb("g_spec", [P, PAIRS, 2, HY_W], F32, s2)
            with ExitStack() as s3:
                sreg = sb("s_blocks", [P, 4, HY_W], F32, s3)
                win = sb("window", [P, 4, HY_W], F32, s3)
            with ExitStack() as s3:
                ureg = sb("u_blocks", [P, 5, HY_W], F32, s3)
                ufold = sb("u_fold", [P, 2, HY_W], F32, s3)
            yhi = sb("y_hi", [P, 2, 2, HY_W], F32R, s2)
            ylo = sb("y_lo", [P, 2, 2, HY_W], F32R, s2)
    with ExitStack() as s:
        sb("attn_space", [P, 4 * ROW], F32, s)
        with ExitStack() as s2:
            mlb = sb("merged_lo_end", [P, 2, ROW], F32R, s2)
        sb("k_v_space2", [P, KV_SPACE], F32, s)
        sb("attn_lo_space", [P, 4 * ROW], F32, s)
        mhi = sb("merged_hi", [P, KD, ROW], F32R, s)
        sb("hy_space", [P, 8 * ROW], F32, s)
        mla = sb("merged_lo", [P, KD - 2, ROW], F32R, s)
    with ExitStack() as s:
        sums = sb("sums", [P, 2, ROW], F32, s)
        sq = sb("squares", [P, 2, ROW], F32, s)
        acth = sb("act_hi", [P, FH, ROW], F32R, s)
        actl = sb("act_lo", [P, FH, ROW], F32R, s)
        gz = sb("gate_rows", [P, 2, ROW], F32, s)
        ga = sb("gate_acc", [P, 2, ROW], F32, s)
        with ExitStack() as s2:
            crow = sb("cond_by_row", [P, 2, D_MODEL], F32, s2)
        diag = sb("diag", [P, 2 * NB, P], F32, s)

    def mlo(d):
        return mla[:, d, :] if d < KD - 2 else mlb[:, d - KD + 2, :]

    gp = st.enter_context(nc.psum_tensor("gemm_psum", [P, 4, 512], F32))
    ax = st.enter_context(nc.psum_tensor("aux_psum", [P, 4, 512], F32))

    def pair(i):
        return gp[:, 2 * (i % 2):2 * (i % 2) + 2, 0:HALF]

    mlp_bank = lambda n: ax[:, 0, :] if n == 2 else gp[:, 2 + n, :]
    ADA_AT = 384

    def two(row):
        return row.rearrange("p (a b) -> p a b", a=2)

    def tok(b):
        at = C0 if b == 0 else L0 + P * (b - 1)
        return slice(at, at + P)

    scf = sc[:, :, :].rearrange("p a b -> p (a b)")
    vrow = scf[:, 0:ROW]
    parc = lambda name, i: par[:, PAR[name] + i:PAR[name] + i + 1]
    cache_k = par[:, PAR["cache_k"]:PAR["cache_k"] + P]
    cache_v = par[:, PAR["cache_v"]:PAR["cache_v"] + P]
    f32 = lambda ap: ap.bitcast(F32)

    TILES, last_read, n_of = [], [], {}
    for g, (kind, i) in enumerate(GEMM):
        for c in range({"F": 0, "I": 0, "k": 1, "v": 1, "down": 1}.get(kind, 2)):
            TILES.append((g, c))
            n = n_of[kind] = n_of.get(kind, 0) + 1
            last_read.append({
                "q": ("qkv_out", n), "k": ("qkv_out", 5), "v": ("qkv_out", 6), "z": ("z_acc", n),
                "gate": ("gate_out", n), "proj": ("proj_out", n), "out": ("out_out", n),
                "up": (("up_acc", (n + 1) // 2), ("up_out", n // 2))[c],
                "down": ("down_out", n)}[kind])
    n_of, chunk_done = {}, []
    for kind, i in GEMM:
        if kind in "FI":
            chunk_done.append(None)
            continue
        ev = "qkv_mm" if kind in "qkv" else kind + "_mm"
        n_of[ev] = n_of.get(ev, 0) + {"k": 1, "v": 1, "down": 1}.get(kind, 2)
        chunk_done.append((ev, n_of[ev]))
    gF = at_g("F", 0)
    STREAM = stream()
    STEP = {item: n for n, item in enumerate(STREAM)}
    chunk_done[gF:gF + 6] = [("gsp_mm", 6), ("gsp_mm", 10), ("cinv_mm", 1), ("linv_mm", 2),
                             ("usp_mm", 10), ("linv_mm", 4)]
    G_V = [(0, 1), (2, 3), (4, 5), (6, 7, 8, 9), (6, 7, 8, 9)]
    U_V = [(0, 0)] + G_V[1:]
    Y_SLOT = [0, 1, 0, 1, 0]
    GS_V = [0, 1, 6, 7, 8, 9, 2, 3, 4, 5]
    US_V = [0, 6, 7, 8, 9, 2, 3, 4, 5]
    key_blocks = [[(kd, f + i) for kd, f, m in ks for i in range(m)] for ks in KEYS]
    mm, tr = nc.tensor.matmul, nc.tensor.transpose
    block = st.enter_context(nc.Block())

    @block.sync
    def _(sp):
        lane = Counts(None)
        due = lane.due
        sp.dma_start(cs[:, :, :], A["cond"]).then_inc(sem["cond_in"], 16)
        for n, (L, what, i) in enumerate(STREAM):
            lane.start(L)
            if n == 2:
                sp.dma_start(ident[:, :], A["ident"]).then_inc(sem["x_in"], 16)
                sp.dma_start(xin[:, 0, :], A["x_prompt"][0]).then_inc(sem["x_in"], 16)
                sp.dma_start(xin[:, 1:NB, :], A["x_sample"][0].rearrange("(b p) d -> p b d", p=P))\
                    .then_inc(sem["x_in"], 16)
                for dst, src in ((feat, "feat"), (w1, "w1"), (w2, "w2"), (mlpv, "mlpv"), (rot, "rot"),
                                 (ones, "ones"), (mask_in, "mask")):
                    sp.dma_start(dst[:, :], A[src]).then_inc(sem["consts_in"], 16)
            if n >= 2:
                before = STREAM[n - 2]
                if before[1] == "ada" and before[0] == 0:
                    sp.wait_ge(sem["ada_mm"], 2 * (before[2] + 1))
                elif before[1] == "ada":
                    sp.wait_ge(sem["ada_t"], 4 * (ADA_STEPS * (before[0] - 1) + before[2] + 1))
                else:
                    sp.wait_ge(sem["w_split"], NG * before[0] + CREDIT["w_split"] + before[2] + 1)
            if what == "ada":
                src, w = A["ada"][i] if L == 0 else A["ada_t"][L - 1, i], CHUNK
            elif GEMM[i][0] in "FI":
                src, w = A["".join(map(str, GEMM[i]))], width(i)
            else:
                src, w = A["w_" + GEMM[i][0]][L, GEMM[i][1]], width(i)
            sp.dma_start(raw[n % 2][:, 0:w], src).then_inc(sem[f"raw{n % 2}"], 16)
        for b in range(NB):
            sp.wait_ge(sem["y_out"], b + 1)
            dst = A["y_prompt"][0] if b == 0 else A["y_sample"][0, P * (b - 1):P * b, :]
            sp.dma_start(dst, yout[:, b % 2, :]).then_inc(sem["y_dma"], 16)
            sp.wait_ge(sem["y_dma"], 16 * (b + 1))

    @block.tensor
    def _(pe):
        pe.sem_inc(sem["down_mm"], CREDIT["down_mm"])
        def ada(t):
            n = STEP[(0, "ada", t // 2)]
            pe.wait_ge(sem[f"raw{n % 2}"], 16 * (n // 2 + 1))
            for kk in range(KD):
                last = mm(gp[0:2, t % 2, ADA_AT:ADA_AT + P], cs[:, kk, :],
                          raw[n % 2][:, P * (KD * (t % 2) + kk):P * (KD * (t % 2) + kk + 1)],
                          start=kk == 0, stop=kk == KD - 1)
            last.then_inc(sem["ada_mm"], 1)

        pe.wait_ge(sem["cond_ready"], 1)
        for t in range(4):
            if t >= 2:
                pe.wait_ge(sem["row_first"], t - 1)
            ada(t)
        pe.wait_ge(sem["x_in"], 16 * 3)
        for d in range(KD):
            if d >= 2:
                pe.wait_ge(sem["x_row"], 2 * (d - 1))
            for b in range(NB):
                o = ax[:, 2 * (d % 2), 0:P] if b == 0 else ax[:, 2 * (d % 2) + 1, P * (b - 1):P * b]
                last = tr(o, xin[:, b, P * d:P * (d + 1)], ident[:, :])
            last.then_inc(sem["x_tr"], 1)
        cols = [(0, 512), (512, 1024), (1024, NT)]
        pe.wait_ge(sem["consts_in"], 16 * 7)
        for lay, (lhs, rhs) in enumerate(((w1, feat), (w2, h1T))):
            for n, (a, b) in enumerate(cols):
                if lay:
                    pe.wait_ge(sem["mlp_sin"], n + 1)
                elif n == 2:
                    pe.wait_ge(sem["x_row"], 16)
                mm(mlp_bank(n)[:, 0:b - a], lhs[:, :], rhs[:, a:b], start=True, stop=True)\
                    .then_inc(sem["mlp_mm"], 1)
                for t in range(4 + 2 * (3 * lay + n), 6 + 2 * (3 * lay + n)):
                    pe.wait_ge(sem["row_first"], t - 1)
                    ada(t)
        for t in range(4 * ADA_GROUP):
            pe.wait_ge(sem["row_first"], t + 1)
            tr(ax[:, 3, 2 * t:2 * t + 2], rows0[0:2, t, :], ident[0:2, 0:2]).then_inc(sem["col_mm"], 1)
        pe.wait_ge(sem["mlp_sin"], 6)
        lane = Counts(None)
        due, raised, now = lane.due, lane.raised, lane.now

        def passes(slot, off, n, hi, lo, out, start, stop, last_event=None):
            pass

        def tile(g, c, blocks, off, moving, event, ready=None):
            t = TILES.index((g, c))
            if t >= 2:
                ev, n = last_read[t - 2]
                pe.wait_ge(sem[ev], due(ev, n))
            s = g % 2
            for kk in range(blocks):
                if ready:
                    ready(kk)
                for n, (w, lo) in enumerate(((whi[s], False), (whi[s], True), (wlo[s], False))):
                    for hf in range(2):
                        last = mm(gp[:, 2 * (t % 2) + hf, 0:HALF],
                                  w[:, off + P * kk:off + P * (kk + 1)],
                                  moving(kk, lo)[:, hf * HALF:(hf + 1) * HALF],
                                  start=kk == 0 and n == 0, stop=kk == blocks - 1 and n == 2)
            last.then_inc(sem[event], raised(event))

        h_mov = lambda kk, lo: (hlo if lo else hhi)[:, kk, :]

        def h_gemm(g, tiles, event, base=None):
            pe.wait_ge(sem["w_split"], due("w_split", g + 1))
            for c in range(tiles):
                ready = (lambda kk: pe.wait_ge(sem["h_ready"], due("h_ready", base + kk + 1))) if base is not None and c == 0 else None
                tile(g, c, KD, c * KD * P, h_mov, event, ready)

        def qk(b):
            for n in range(NH):
                j, gr = n // 2, n % 2
                seq = NH * b + n
                if seq >= 4:
                    pe.wait_ge(sem["qk_out"], due("qk_out", seq - 3))
                if b and n == 3:
                    pe.wait_ge(sem["at_lo"], due("at_lo", b))
                pr = slice(HD * gr, HD * (gr + 1))
                at = 0
                for kd, f, m in KEYS[b]:
                    rhs = {"own": lambda: k[pr, 0, CTX], "ctx": lambda: kcT[pr, :],
                           "lat": lambda: k[pr, 0, L0 + P * f:L0 + P * (f + m)]}[kd]()
                    last = mm(ax[:, n % 4, at:at + P * m], q[pr, j, tok(b)], rhs, start=True, stop=True)
                    at += P * m
                last.then_inc(sem["qk_mm"], raised("qk_mm"))

        row_out = lambda t: "row_dve" if t % 2 else "row_act"

        def ada_col(t):
            pe.wait_ge(sem[row_out(t)], (t - 2 * ADA_FIRST) // 2 + 1)
            at = ADA_AT + 2 * (t % NH)
            tr(gp[:, 2, at:at + 2], rows[0:2, t % 2, :], ident[0:2, 0:2]).then_inc(sem["col_mm"], 1)

        def tpv(b):
            nk = len(key_blocks[b])

            def pv(n):
                seq = NH * b + n
                pe.wait_ge(sem["pt_dve" if n % 2 else "pt_act"], due("pt_dve" if n % 2 else "pt_act", (NH // 2) * b + n // 2 + 1))
                if n == 0 and b:
                    pe.wait_ge(sem["osb_out"], due("osb_out", b))
                for kb, (kd, i) in enumerate(key_blocks[b]):
                    v = cache_v if kd == "ctx" else vtok[:, 0 if kd == "own" else 1 + i, :]
                    last = mm(ax[:, 2, HD * n:HD * (n + 1)], pt[:, n % 2, P * kb:P * (kb + 1)],
                              v[:, HD * (n % 2):HD * (n % 2 + 1)], start=kb == 0, stop=kb == nk - 1)
                last.then_inc(sem["pv_mm"], raised("pv_mm"))

            if L == 0 and b < 4:
                pe.wait_ge(sem["z_acc"], due("z_acc", 2 * b + 6))
            for n in range(NH):
                pe.wait_ge(sem["exp_out"], due("exp_out", NH * b + n + 1))
                if n >= 2:
                    pe.wait_ge(sem["pt_dve" if n % 2 else "pt_act"], due("pt_dve" if n % 2 else "pt_act", (NH // 2) * b + n // 2))
                for kb in range(nk):
                    last = tr(ax[:, n % 2, P * kb:P * (kb + 1)], sc[:, n, P * kb:P * (kb + 1)], ident[:, :])
                last.then_inc(sem["pt_mm"], raised("pt_mm"))
                if L == 0 and b < 4:
                    t = 2 * ADA_FIRST + NH * b + n
                    if n >= 2:
                        pe.wait_ge(sem[row_out(t)], (t - 2 * ADA_FIRST) // 2)
                    ada(t)
                    if n:
                        ada_col(t - 1)
                if n:
                    pv(n - 1)
            pv(NH - 1)
            if L == 0 and b < 4:
                ada_col(2 * ADA_FIRST + NH * b + NH - 1)
            pe.wait_ge(sem["osb_out"], due("osb_out", b + 1))
            for j in range(4):
                last = tr(ax[:, 3, P * j:P * (j + 1)], osb[:, P * j:P * (j + 1)], ident[:, :])
            last.then_inc(sem["ot_mm"], raised("ot_mm"))

        def spectrum(pair_, places, bank, event):
            s = (gF if event == "gsp_mm" else gF + 2) % 2 if pair_ < 3 else \
                (gF + 1 if event == "gsp_mm" else gF + 4) % 2
            nk = len(places)
            for o in range(2):
                r = 2 * pair_ + o
                if r >= 4:
                    pe.wait_ge(sem[event.replace("mm", "out")], due(event.replace("mm", "out"), r - 3))
                for kb, pl in enumerate(places):
                    blk = (4 * pair_ + 2 * o + kb) if pair_ < 3 else (8 * (pair_ - 3) + 4 * o + kb)
                    cols_ = slice(P * blk, P * (blk + 1))
                    for n, (w, v) in enumerate(((whi, vhi), (whi, vlo), (wlo, vhi))):
                        last = mm(bank[:, r % 4, :], w[s][:, cols_], v[:, pl, :],
                                  start=kb == 0 and n == 0, stop=kb == nk - 1 and n == 2)
                last.then_inc(sem[event], raised(event))

        def inverse(pair_, slot, first, final):
            ys = Y_SLOT[pair_]
            pe.wait_ge(sem["y_ready"], due("y_ready", 2 * pair_ + 2))
            for j in range(NHY):
                for o in range(2):
                    at = 512 * (2 * ((pair_ - 1) % 2) + o)
                    for n, (y, w) in enumerate(((yhi, whi), (yhi, wlo), (ylo, whi))):
                        last = mm(ax[:, j, :], y[:, ys, o, P * j:P * (j + 1)], w[slot][:, at:at + 512],
                                  start=first and o == 0 and n == 0, stop=final and o == 1 and n == 2)
            last.then_inc(sem["linv_mm"], raised("linv_mm"))

        def layer_norm(w):
            pe.wait_ge(sem["sum1_out"], due("sum1_out", KD * (w + 1)))
            pe.wait_ge(sem["sum2_out"], due("sum2_out", KD * (w + 1)))
            for i in range(2):
                for b in range(NB):
                    last = mm(ax[:, 3, NB * i + b:NB * i + b + 1], sums[:, i, tok(b)], ones[:, 0:1],
                              start=True, stop=True)
            last.then_inc(sem["stat_mm"], raised("stat_mm"))
            pe.wait_ge(sem["diag_out"], due("diag_out", w + 1))
            for i in range(2):
                for b in range(NB):
                    o = ax[:, 2, P * i:P * (i + 1)] if b == 0 else ax[:, i, P * (b - 1):P * b]
                    last = mm(o, ones[:, :], diag[:, NB * i + b, :], start=True, stop=True)
            last.then_inc(sem["bc_mm"], raised("bc_mm"))

        for L in range(DEPTH):
            lane.start(L)
            h_gemm(0, 2, "qkv_mm", base=0)
            h_gemm(1, 2, "qkv_mm")
            h_gemm(2, 1, "qkv_mm")
            h_gemm(3, 1, "qkv_mm")
            h_gemm(4, 2, "z_mm")
            for r in range(5):
                pe.wait_ge(sem["qkv_out"], due("qkv_out", r + 1))
                if r == 4:
                    pe.wait_ge(sem["rot_out"], due("rot_out", 1))
                src = q[:, r, LAT] if r < 4 else k[:, 0, LAT]
                mm(ax[:, r % 4, :], rot[:, :], src, start=True, stop=True).then_inc(sem["rot_mm"], raised("rot_mm"))
            pe.wait_ge(sem["qkv_out"], due("qkv_out", 6))
            pe.wait_ge(sem["rot_out"], due("rot_out", 3))
            for b in range(1, NB):
                last = tr(ax[:, 1, P * (b - 1):P * b], vrow[:, tok(b)], ident[:, :])
            last.then_inc(sem["vt_mm"], raised("vt_mm"))
            tr(ax[:, 2, 0:P], vrow[:, CTX], ident[:, :])
            tr(ax[:, 2, P:2 * P], cache_k, ident[:, :])
            tr(ax[:, 2, 2 * P:3 * P], k[:, 0, CTX], ident[:, :]).then_inc(sem["vt_mm"], raised("vt_mm"))
            h_gemm(5, 2, "z_mm")
            pe.wait_ge(sem["rot_out"], due("rot_out", 5))
            pe.wait_ge(sem["vt_out"], due("vt_out", 4))
            for b in range(NB):
                if b:
                    if L == 0 and b > 1:
                        pe.wait_ge(sem["mod_done"], due("mod_done", b + 1))
                    h_gemm(5 + b, 2, "z_mm")
                    tpv(b - 1)
                qk(b)
            tpv(NB - 1)
            pe.wait_ge(sem["mod_done"], due("mod_done", 6))
            pe.wait_ge(sem["at_lo"], due("at_lo", NB))
            pe.wait_ge(sem["w3_in"], due("w3_in", 16))
            for n in range(10):
                if n >= 4:
                    pe.wait_ge(sem["filt_out"], due("filt_out", n - 3))
                at = P * n if n < 2 else (2 * P if n % 2 == 0 else 2 * P + DEC_SEQ) + P * (n // 2 - 1)
                mm(ax[:, n % 4, :], h2T[:, at:at + P], w3[:, HY_W * (n % 2):HY_W * (n % 2 + 1)],
                           start=True, stop=True).then_inc(sem["filt_mm"], raised("filt_mm"))
            pe.wait_ge(sem["filt_out"], due("filt_out", 10))
            pe.wait_ge(sem["w_split"], due("w_split", gF + 1))
            pe.wait_ge(sem["gs_ready"], due("gs_ready", 2))
            for p_ in range(PAIRS):
                if p_ == 1:
                    pe.wait_ge(sem["gs_ready"], due("gs_ready", 10))
                if p_ == 3:
                    pe.wait_ge(sem["w_split"], due("w_split", gF + 2))
                spectrum(p_, G_V[p_], ax, "gsp_mm")
            pe.wait_ge(sem["gsp_out"], due("gsp_out", 10))
            pe.wait_ge(sem["xu_ready"], due("xu_ready", 4))
            for b in range(NB):
                if b == 4:
                    pe.wait_ge(sem["ut_out"], due("ut_out", 1))
                for j in range(NHY):
                    last = tr(ax[:, b % 4, P * j:P * (j + 1)], xu[:, j, tok(b)], ident[:, :])
                last.then_inc(sem["ut_mm"], raised("ut_mm"))
            pe.wait_ge(sem["w_split"], due("w_split", gF + 3))
            pe.wait_ge(sem["us_ready"], due("us_ready", 1))
            pe.wait_ge(sem["z_acc"], due("z_acc", 12))
            for p_ in range(3):
                if p_ == 1:
                    pe.wait_ge(sem["us_ready"], due("us_ready", 9))
                spectrum(p_, U_V[p_], gp, "usp_mm")
            pe.wait_ge(sem["y_ready"], due("y_ready", 2))
            pe.wait_ge(sem["ut_out"], due("ut_out", 5))
            s = (gF + 2) % 2
            for j in range(NHY):
                for o in range(2):
                    cols_ = slice(P * (12 + o), P * (13 + o))
                    for n, (y, w) in enumerate(((yhi, whi), (yhi, wlo), (ylo, whi))):
                        last = mm(ax[:, 0, P * j:P * (j + 1)], y[:, 0, o, P * j:P * (j + 1)], w[s][:, cols_],
                                  start=o == 0 and n == 0, stop=o == 1 and n == 2)
            last.then_inc(sem["cinv_mm"], raised("cinv_mm"))
            pe.wait_ge(sem["cinv_out"], due("cinv_out", 1))
            pe.wait_ge(sem["w_split"], due("w_split", gF + 4))
            inverse(1, (gF + 3) % 2, True, False)
            inverse(2, (gF + 3) % 2, False, False)
            pe.wait_ge(sem["w_split"], due("w_split", gF + 5))
            spectrum(3, U_V[3], gp, "usp_mm")
            spectrum(4, U_V[4], gp, "usp_mm")
            pe.wait_ge(sem["w_split"], due("w_split", gF + 6))
            inverse(3, (gF + 5) % 2, False, False)
            inverse(4, (gF + 5) % 2, False, True)
            for m in range(KD):
                g = at_g("gate", m)
                h_gemm(g, 2, "gate_mm", base=KD if m == 0 else None)
                if m == 0:
                    pe.wait_ge(sem["hy_ready"], due("hy_ready", 4))
                    pe.wait_ge(sem["pads_at"], due("pads_at", 1))
                pe.wait_ge(sem["w_split"], due("w_split", g + 2))
                tile(g + 1, 0, 4, 0, lambda kk, lo: (atl if lo else ath)[:, kk, :], "proj_mm")
                tile(g + 1, 1, 4, 4 * P, lambda kk, lo: (hyl if lo else hyh)[:, kk, :], "proj_mm")
            for i in range(4):
                g = at_g("out", i)
                pe.wait_ge(sem["w_split"], due("w_split", g + 1))
                for c in range(2):
                    tile(g, c, KD, c * KD * P, lambda kk, lo: mlo(kk) if lo else mhi[:, kk, :], "out_mm",
                         (lambda kk: pe.wait_ge(sem["m_ready"], due("m_ready", kk + 1))) if i == 0 and c == 0 else None)
            layer_norm(0)
            for hf in range(2):
                for j in range(FH):
                    jj = FH * hf + j
                    h_gemm(at_g("up", jj), 2, "up_mm", base=2 * KD if jj == 0 else None)
                for m in range(KD):
                    g = at_g("down", KD * hf + m)
                    pe.wait_ge(sem["w_split"], due("w_split", g + 1))
                    tile(g, 0, FH, 0, lambda kk, lo: (actl if lo else acth)[:, kk, :], "down_mm",
                         (lambda kk: pe.wait_ge(sem["act_ready"], due("act_ready", FH * hf + kk + 1))) if m == 0 else None)
            layer_norm(1)
            lane.end()
        for b in range(NB):
            pe.wait_ge(sem["ln_x"], due("ln_x", 16))
            pe.wait_ge(sem["ln_norm"], due("ln_norm", 16))
            if b >= 2:
                pe.wait_ge(sem["y_out"], b - 1)
            for d in range(KD):
                last = tr(ax[:, 2 * (b % 2) + d // 4, P * (d % 4):P * (d % 4 + 1)], x[:, d, tok(b)], ident[:, :])
            last.then_inc(sem["y_mm"], 1)

    @block.scalar
    def _(act):
        lane = Counts("act_order")
        due, raised, now = lane.due, lane.raised, lane.now
        run = nc.scalar.activation
        act.sem_inc(sem["ln_x"], CREDIT["ln_x"])
        act.wait_ge(sem["cond_in"], 16)
        run(cs[:, :, :], cs[:, :, :], ACT.Silu).then_inc(sem["cond_ready"], 1)

        def first_rows(a, b):
            for t in range(a, b):
                act.wait_ge(sem["ada_mm"], t + 1)
                run(rows0[0:2, t, :], gp[0:2, t % 2, ADA_AT:ADA_AT + P], ACT.Copy).then_inc(sem["row_first"], 1)

        def sine(i):
            dst = (h1T, h2T)[i // 3]
            a, b = ((0, 512), (512, 1024), (1024, NT))[i % 3]
            act.wait_ge(sem["mlp_arg"], i + 1)
            run(dst[:, a:b], dst[:, a:b], ACT.Sin).then_inc(sem["mlp_sin"], 1)

        first_rows(0, 6)
        for i in range(5):
            first_rows(6 + 2 * i, 8 + 2 * i)
            sine(i)
        sine(5)

        def split(g):
            s = g % 2
            n = width(g)
            st_ = STEP[(L, "g", g)]
            act.wait_ge(sem[f"raw{st_ % 2}"], 16 * (st_ // 2 + 1))
            if g >= 2:
                ev, m = chunk_done[g - 2]
                act.wait_ge(sem[ev], due(ev, m))
            else:
                act.wait_ge(sem["down_mm"], due("down_mm", g - 1))
            run(whi[s][:, 0:n], raw[st_ % 2][:, 0:n], ACT.Copy).then_inc(sem["w_hi"], raised("w_hi"))

        def hi(dst, src, ready, n, event):
            act.wait_ge(sem[ready], due(ready, n))
            run(dst, src, ACT.Copy).then_inc(sem[event], raised(event))

        def soft(b):
            nk = len(key_blocks[b]) * P
            act.wait_ge(sem["soft_m"], due("soft_m", b + 1))
            run(small[:, 32:40], small[:, 24:32], ACT.Exp).then_inc(sem["act_order"], raised("act_order"))
            for n in range(NH):
                run(sc[:, n, 0:nk], sc[:, n, 0:nk], ACT.Exp, bias=small[:, 16 + n:17 + n],
                       scale=HD ** -0.5, accum_out=small[:, 40 + n:41 + n]).then_inc(sem["exp_out"], raised("exp_out"))

        def tpv(b):
            nk = len(key_blocks[b]) * P
            for n in range(0, NH, 2):
                act.wait_ge(sem["pt_mm"], due("pt_mm", NH * b + n + 1))
                if NH * b + n >= 2:
                    act.wait_ge(sem["pv_mm"], due("pv_mm", NH * b + n - 1))
                run(pt[:, 0, 0:nk], ax[:, 0, 0:nk], ACT.Copy).then_inc(sem["pt_act"], raised("pt_act"))
                if L == 0 and b < 4:
                    t = 2 * ADA_FIRST + NH * b + n
                    act.wait_ge(sem["ada_mm"], t + 1)
                    if t >= 2 * ADA_FIRST + 2:
                        act.wait_ge(sem["col_mm"], t - 1)
                    run(rows[0:2, 0, :], gp[0:2, 0, ADA_AT:ADA_AT + P], ACT.Copy).then_inc(sem["row_act"], 1)
            act.wait_ge(sem["ot_mm"], due("ot_mm", b + 1))
            run(ath[:, :, tok(b)], ax[:, 3, :].rearrange("p (j t) -> p j t", j=4), ACT.Copy).then_inc(sem["at_hi"], raised("at_hi"))

        def squares(m, event, n):
            act.wait_ge(sem[event], due(event, n))
            k_ = n_sq[0]
            n_sq[0] += 1
            if k_ >= 2:
                act.wait_ge(sem["sum2_out"], due("sum2_out", k_ - 1))
            run(sq[:, m % 2, :], x[:, m, :], ACT.Square).then_inc(sem["sq_out"], raised("sq_out"))

        for L in range(DEPTH):
            lane.start(L)
            n_sq = [0]
            act.wait_ge(sem["params_in"], due("params_in", 16))
            split(0)
            for d in range(KD):
                hi(hhi[:, d, :], hsrc[:, d % 2, :], "h_src", d + 1, "h_hi")
            for g in range(4):
                split(g + 1)
                for t in ((0, 1), (2, 3), (4,), (5,))[g]:
                    act.wait_ge(sem["qkv_mm"], due("qkv_mm", t + 1))
                    dst = q[:, t, :] if t < 4 else k[:, 0, :] if t == 4 else vrow
                    run(two(dst), pair(t), ACT.Copy).then_inc(sem["qkv_out"], raised("qkv_out"))
            for i in range(6):
                split(5 + i)
                for c in range(2):
                    t = 2 * i + c
                    act.wait_ge(sem["z_mm"], due("z_mm", t + 1))
                    if i:
                        act.wait_ge(sem["z_out"], due("z_out", 2 * i))
                        if i < 5:
                            act.wait_ge(sem["xu_ready"], due("xu_ready", i))
                    src = pair(t)
                    run(two(zt[:, c, :]), src, ACT.Copy).then_inc(sem["z_raw"], raised("z_raw"))
                    dst = ca[:, c, :] if i < 4 else x0c[:, 2 * (i - 4) + c, :]
                    zi = (4 + i, 8 + i)[c] if i < 4 else 2 * (i - 4) + c
                    run(two(dst), src, ACT.Identity, bias=parc("hy_b", zi),
                           scale=parc("hy_w", 3 * zi + 1)).then_inc(sem["z_acc"], raised("z_acc"))
                if i == 0:
                    act.wait_ge(sem["vt_mm"], due("vt_mm", 1))
                    run(vtok[:, 1:NB, :], ax[:, 1, :].rearrange("p (b t) -> p b t", t=P), ACT.Copy).then_inc(sem["vt_out"], raised("vt_out"))
                    act.wait_ge(sem["vt_mm"], due("vt_mm", 2))
                    run(vtok[:, 0, :], ax[:, 2, 0:P], ACT.Copy).then_inc(sem["vt_out"], raised("vt_out"))
                    run(kcT[:, :], ax[:, 2, P:2 * P], ACT.Copy).then_inc(sem["vt_out"], raised("vt_out"))
                    run(kout[:, :], ax[:, 2, 2 * P:3 * P], ACT.Copy).then_inc(sem["vt_out"], raised("vt_out"))
                else:
                    if i >= 2:
                        tpv(i - 2)
                    soft(i - 1)
            tpv(4)
            split(gF + 1)
            act.wait_ge(sem["z_mm"], due("z_mm", 12))
            fsrc = [sreg[:, 0, :], dreg[:, :]] + [dreg[:, :]] * 4 + [prod[:, 0, :], prod[:, 1, :]] * 2
            for n, v in enumerate(GS_V):
                hi(vhi[:, v, :], fsrc[n], "gs_src", n + 1, "gs_hi")
            for r in range(10):
                act.wait_ge(sem["gsp_mm"], due("gsp_mm", r + 1))
                run(gsp[:, r // 2, r % 2, :], ax[:, r % 4, :], ACT.Copy).then_inc(sem["gsp_out"], raised("gsp_out"))
                if r == 5:
                    split(gF + 2)
            split(gF + 3)
            usrc = [ureg[:, n, :] for n in range(5)] + [ufold[:, 0, :], ufold[:, 1, :]] * 2
            for n, v in enumerate(US_V):
                hi(vhi[:, v, :], usrc[n], "us_src", n + 1, "us_hi")
            for p_ in range(PAIRS):
                for o in range(2):
                    r = 2 * p_ + o
                    act.wait_ge(sem["usp_mm"], due("usp_mm", r + 1))
                    if p_:
                        act.wait_ge(sem["y_ready"], due("y_ready", 2 * p_))
                    run(us[:, o, :], gp[:, r % 4, :], ACT.Copy).then_inc(sem["usp_out"], raised("usp_out"))
                for o in range(2):
                    if p_ == 2:
                        act.wait_ge(sem["cinv_mm"], due("cinv_mm", 1))
                    if p_ >= 3:
                        act.wait_ge(sem["linv_mm"], due("linv_mm", p_ - 2))
                    hi(yhi[:, Y_SLOT[p_], 1 - o, :], us[:, o, :], "y_src", 2 * p_ + o + 1, "y_hi")
                if p_ == 2:
                    split(gF + 4)
                if p_ == 3:
                    split(gF + 5)
            split(gF + 6)
            act.wait_ge(sem["usp_mm"], due("usp_mm", 10))
            for d in range(KD):
                hi(hhi[:, d, :], hsrc[:, d % 2, :], "h_src", KD + d + 1, "h_hi")
            for j in range(NHY):
                hi(hyh[:, j, :], xu[:, j, :], "hy_src", j + 1, "hy_hi")
            for m in range(KD):
                g = at_g("gate", m)
                split(g + 1)
                for c in range(2):
                    act.wait_ge(sem["gate_mm"], due("gate_mm", 2 * m + c + 1))
                    act.wait_ge(sem["m_ready"], due("m_ready", m)) if m else act.wait_ge(sem["h_ready"], due("h_ready", 2 * KD))
                    t = TILES.index((g, c))
                    run(two(gates[:, c, :]), pair(t), ACT.Sigmoid).then_inc(sem["gate_out"], raised("gate_out"))
                split(g + 2)
                hi(mhi[:, m, :], gates[:, 0, :], "m_src", m + 1, "m_hi")
            for i in range(4):
                split(at_g("out", i) + 1)
                for c in range(2):
                    squares(2 * i + c, "out_out", 2 * i + c + 1)
            for w in range(2):
                act.wait_ge(sem["ln_var"], due("ln_var", w + 1))
                run(small[:, 71:76], small[:, 66:71], ACT.Sqrt).then_inc(sem["ln_sqrt"], raised("ln_sqrt"))
                for d in range(KD + (w == 0)):
                    if d < KD:
                        act.wait_ge(sem["ln_norm"], due("ln_norm", KD * w + d + 1))
                        ln = f"ln{w + 1}_"
                        run(x[:, d, :], x[:, d, :], ACT.Identity, bias=parc(ln + "b", d),
                               scale=parc(ln + "g", d)).then_inc(sem["ln_x"], raised("ln_x"))
                    if w == 0 and d:
                        hi(hhi[:, d - 1, :], hsrc[:, (d - 1) % 2, :], "h_src", 2 * KD + d, "h_hi")
                if w:
                    break
                if L + 1 < DEPTH:
                    act.wait_ge(sem["cond_rows_in"], 16 * (L + 1))
                    run(crow[:, :, :], crow[:, :, :], ACT.Silu).then_inc(sem["cond_rows"], 1)
                for hf in range(2):
                    for j in range(FH):
                        jj = FH * hf + j
                        g = at_g("up", jj)
                        split(g + 1)
                        sl = jj % 2
                        src = pair(TILES.index((g, 0)))
                        act.wait_ge(sem["up_mm"], due("up_mm", 2 * jj + 1))
                        if jj >= 2:
                            act.wait_ge(sem["act_ready"], due("act_ready", jj - 1))
                        run(two(gz[:, sl, :]), src, ACT.Copy).then_inc(sem["up_raw"], raised("up_raw"))
                        run(two(ga[:, sl, :]), src, ACT.Identity, bias=parc("ff_b", jj),
                               scale=parc("ff_w", 3 * jj + 1)).then_inc(sem["up_acc"], raised("up_acc"))
                        act.wait_ge(sem["up_taps"], due("up_taps", jj + 1))
                        run(ga[:, sl, :], ga[:, sl, :], ACT.Gelu).then_inc(sem["up_gelu"], raised("up_gelu"))
                        if hf and j == 0:
                            act.wait_ge(sem["down_mm"], due("down_mm", KD))
                        hi(acth[:, j, :], ga[:, sl, :], "up_out", jj + 1, "act_hi")
                    for m in range(KD):
                        g = at_g("down", KD * hf + m)
                        if g + 1 < NG:
                            split(g + 1)
                        if hf:
                            squares(m, "down_out", KD + m + 1)
            lane.end()

    @block.vector
    def _(dve):
        lane = Counts("dve_order")
        due, raised, now = lane.due, lane.raised, lane.now
        V = nc.vector
        TT, TS, STT = V.tensor_tensor, V.tensor_scalar, V.scalar_tensor_tensor
        for n in ("w_split", "m_ready", "h_ready"):
            dve.sem_inc(sem[n], CREDIT[n])
        dve.wait_ge(sem["consts_in"], 16 * 7)
        V.tensor_copy(mask[:, :], mask_in[:, :]).then_inc(sem["mask_done"], 1)
        dve.wait_ge(sem["mask_done"], 1)
        dve.wait_ge(sem["x_zero"], 1)
        for d in range(KD):
            dve.wait_ge(sem["x_tr"], d + 1)
            V.tensor_copy(x[:, d, CTX], ax[:, 2 * (d % 2), 0:P]).then_inc(sem["x_row"], 1)
            V.tensor_copy(x[:, d, LAT], ax[:, 2 * (d % 2) + 1, :]).then_inc(sem["x_row"], 1)
        n_ord = 0
        for lay, dst in enumerate((h1T, h2T)):
            for n, (a, b) in enumerate(((0, 512), (512, 1024), (1024, NT))):
                dve.wait_ge(sem["mlp_mm"], 3 * lay + n + 1)
                arg, turns = dst[:, a:b], prod[:, 0, 0:b - a]
                ops = [lambda: TS(arg, mlp_bank(n)[:, 0:b - a], mlpv[:, 2 * lay:2 * lay + 1],
                                  mlpv[:, 2 * lay + 1:2 * lay + 2], ALU.add, ALU.mult),
                       lambda: TS(turns, arg, 1 / (2 * math.pi), MAGIC, ALU.mult, ALU.add),
                       lambda: TS(turns, turns, -MAGIC, None, ALU.add)]
                ops += [lambda c=c: STT(arg, turns, -c, arg, ALU.mult, ALU.add) for c in TWO_PI_PARTS]
                for op in ops:
                    op().then_inc(sem["mlp_order"], 1)
                    n_ord += 1
                    dve.wait_ge(sem["mlp_order"], n_ord)
                TS(arg, arg, 3.1415925, -3.1415925, ALU.min, ALU.max).then_inc(sem["mlp_arg"], 1)
        dve.wait_ge(sem["mlp_arg"], 6)

        def modulation(v, sums_):
            b_ada = par[:, PAR["b_ada"] + KD * v:PAR["b_ada"] + KD * (v + 1)].unsqueeze(2).to_broadcast([P, KD, 2])
            STT(mod[:, KD * v:KD * (v + 1), :], sums_.rearrange("p (j g) -> p j g", g=2),
                float(v in (1, 4)), b_ada, ALU.add, ALU.add).then_inc(sem["mod_done"], raised("mod_done"))

        def ada_t(c):
            n = STEP[(L + 1, "ada", c)]
            dve.wait_ge(sem[f"raw{n % 2}"], 16 * (n // 2 + 1))
            for t in (2 * c, 2 * c + 1):
                for gr in range(2):
                    k_ = 4 * ADA_STEPS * L + 2 * t + gr
                    if 2 * t + gr >= 2:
                        dve.wait_ge(sem["ada_t"], k_ - 1)
                    to = small[:, 2 * (t - G2) + gr:2 * (t - G2) + gr + 1] if t >= G2 else mod[:, t, gr:gr + 1]
                    V.tensor_tensor_reduce(out=ax[:, 2 * gr:2 * gr + 2, :].rearrange("p a b -> p (a b)"),
                                           in0=raw[n % 2][:, D_MODEL * (t % 2):D_MODEL * (t % 2 + 1)],
                                           in1=crow[:, gr, :], scale=1.0, scalar=0.0, op0=ALU.mult,
                                           op1=ALU.add, accum_out=to).then_inc(sem["ada_t"], 1)

        def split(g):
            s, n = g % 2, width(g)
            dve.wait_ge(sem["w_hi"], due("w_hi", g + 1))
            TT(wlo[s][:, 0:n], raw[STEP[(L, "g", g)] % 2][:, 0:n], f32(whi[s][:, 0:n]), ALU.subtract).then_inc(sem["w_split"], raised("w_split"))

        def lo(dst, src, hi_, event_hi, n, event):
            dve.wait_ge(sem[event_hi], due(event_hi, n))
            TT(dst, src, f32(hi_), ALU.subtract).then_inc(sem[event], raised(event))

        def h_src(n, d, sh, sc_):
            if d == 0:
                dve.wait_ge(sem["pads_h"], due("pads_h", n + 1))
            if d >= 2:
                dve.wait_ge(sem["h_ready"], due("h_ready", KD * n + d - 1))
            for gr, cols_ in enumerate((CTX, LAT)):
                TS(hsrc[:, d % 2, cols_], x[:, d, cols_], mod[:, sc_ + d, gr:gr + 1],
                      mod[:, sh + d, gr:gr + 1], ALU.mult, ALU.add).then_inc(sem["h_src" if gr else "dve_order"], raised("h_src" if gr else "dve_order"))

        def h_lo(n, d):
            lo(hlo[:, d, :], hsrc[:, d % 2, :], hhi[:, d, :], "h_hi", KD * n + d + 1, "h_ready")

        def h_all(n, sh, sc_):
            for d in range(KD + 1):
                if d < KD:
                    h_src(n, d, sh, sc_)
                if d:
                    h_lo(n, d - 1)

        def taps(rows, accs, ws, event):
            for tap, a in ((0, 0), (2, 2)):
                for i, (z, acc, w) in enumerate(zip(rows, accs, ws)):
                    if tap and i == 0:
                        dve.wait_ge(sem["dve_order"], now("dve_order"))
                    STT(acc[:, 1:ROW - 1], z[:, a:a + ROW - 2], w(tap), acc[:, 1:ROW - 1],
                           ALU.mult, ALU.add).then_inc(sem[event if tap else "dve_order"], raised(event if tap else "dve_order"))

        def soft(b):
            nk = len(key_blocks[b]) * P
            if b:
                dve.wait_ge(sem["at_lo"], now("at_lo"))
            for n in range(NH):
                dve.wait_ge(sem["qk_mm"], due("qk_mm", NH * b + n + 1))
                V.tensor_tensor_reduce(out=sc[:, n, 0:nk], in0=ax[:, n % 4, 0:nk],
                                          in1=mask[:, P * MASK_AT[b]:P * MASK_AT[b] + nk], scale=1.0,
                                          scalar=-3e38, op0=ALU.add, op1=ALU.max,
                                          accum_out=small[:, n:n + 1]).then_inc(sem["qk_out"], raised("qk_out"))
            dve.wait_ge(sem["qk_out"], now("qk_out"))
            sink = par[:, PAR["sink"]:PAR["sink"] + NH]
            STT(small[:, 8:16], small[:, 0:8], HD ** -0.5, sink, ALU.mult, ALU.max).then_inc(sem["dve_order"], raised("dve_order"))
            dve.wait_ge(sem["dve_order"], now("dve_order"))
            TS(small[:, 16:24], small[:, 8:16], -1.0, None, ALU.mult).then_inc(sem["dve_order"], raised("dve_order"))
            TT(small[:, 24:32], sink, small[:, 8:16], ALU.subtract).then_inc(sem["soft_m"], raised("soft_m"))

        def tpv(b):
            nk = len(key_blocks[b]) * P
            dve.wait_ge(sem["exp_out"], due("exp_out", NH * (b + 1)))
            TT(small[:, 48:56], small[:, 40:48], small[:, 32:40], ALU.add).then_inc(sem["dve_order"], raised("dve_order"))
            dve.wait_ge(sem["dve_order"], now("dve_order"))
            V.reciprocal(small[:, 56:64], small[:, 48:56]).then_inc(sem["dve_order"], raised("dve_order"))
            for n in range(1, NH, 2):
                dve.wait_ge(sem["pt_mm"], due("pt_mm", NH * b + n + 1))
                if NH * b + n >= 2:
                    dve.wait_ge(sem["pv_mm"], due("pv_mm", NH * b + n - 1))
                V.tensor_copy(pt[:, 1, 0:nk], ax[:, 1, 0:nk]).then_inc(sem["pt_dve"], raised("pt_dve"))
                if L == 0 and b < 4:
                    t = 2 * ADA_FIRST + NH * b + n
                    dve.wait_ge(sem["ada_mm"], t + 1)
                    if t >= 2 * ADA_FIRST + 2:
                        dve.wait_ge(sem["col_mm"], t - 1)
                    V.tensor_copy(rows[0:2, 1, :], gp[0:2, 1, ADA_AT:ADA_AT + P]).then_inc(sem["row_dve"], 1)
            dve.wait_ge(sem["pv_mm"], due("pv_mm", NH * (b + 1)))
            if b:
                dve.wait_ge(sem["ot_mm"], due("ot_mm", b))
            TT(osb[:, :].rearrange("p (n d) -> p n d", d=HD),
                  ax[:, 2, :].rearrange("p (n d) -> p n d", d=HD),
                  small[:, 56:64].unsqueeze(2).to_broadcast([P, NH, HD]), ALU.mult).then_inc(sem["osb_out"], raised("osb_out"))
            dve.wait_ge(sem["at_hi"], due("at_hi", b + 1))
            TT(atl[:, :, tok(b)], ax[:, 3, :].rearrange("p (j t) -> p j t", j=4),
                  f32(ath[:, :, tok(b)]), ALU.subtract).then_inc(sem["at_lo"], raised("at_lo"))
            if L == 0 and b < 4:
                dve.wait_ge(sem["col_mm"], 2 * ADA_FIRST + NH * (b + 1))
                modulation(2 + b, gp[:, 2, ADA_AT:ADA_AT + 2 * KD])

        def residual(m, t, gate, event):
            for n, (gr, bank, a, b) in enumerate(((0, 0, C0, C0 + SEQ), (1, 0, L0, HALF), (1, 1, 0, HALF - 1))):
                xs = x[:, m, HALF * bank + a:HALF * bank + b]
                STT(xs, gp[:, 2 * (t % 2) + bank, a:b], mod[:, gate + m, gr:gr + 1], xs,
                       ALU.mult, ALU.add).then_inc(sem[event if n == 2 else "dve_order"], raised(event if n == 2 else "dve_order"))

        def sum2(m, n):
            dve.wait_ge(sem["sq_out"], due("sq_out", n))
            if m == 0:
                V.tensor_copy(sums[:, 1, :], sq[:, 0, :]).then_inc(sem["sum2_out"], raised("sum2_out"))
            else:
                dve.wait_ge(sem["sum2_out"], now("sum2_out"))
                TT(sums[:, 1, :], sums[:, 1, :], sq[:, m % 2, :], ALU.add).then_inc(sem["sum2_out"], raised("sum2_out"))

        for L in range(DEPTH):
            lane.start(L)
            dve.wait_ge(sem["params_in"], due("params_in", 16))
            if L == 0:
                dve.wait_ge(sem["col_mm"], 4 * ADA_GROUP)
                for v in range(2):
                    modulation(v, ax[:, 3, 2 * KD * v:2 * KD * (v + 1)])
            else:
                dve.wait_ge(sem["ada_t"], 4 * ADA_STEPS * L)
                for v in range(6):
                    modulation(v, mod[:, KD * v:KD * (v + 1), :].rearrange("p j g -> p (j g)") if v < 5 else small[:, 0:2 * KD])
            dve.wait_ge(sem["mod_done"], now("mod_done"))
            split(0)
            h_all(0, SH1, SC1)
            for g in range(4):
                split(g + 1)
            for i in range(6):
                split(5 + i)
                dve.wait_ge(sem["z_acc"], due("z_acc", 2 * i + 2))
                if i < 4:
                    taps([zt[:, c, :] for c in range(2)], [ca[:, c, :] for c in range(2)],
                         [lambda tp, z=z: parc("hy_w", 3 * z + tp) for z in (4 + i, 8 + i)], "z_out")
                    dve.wait_ge(sem["z_out"], now("z_out"))
                    TT(xu[:, i, :], ca[:, 0, :], ca[:, 1, :], ALU.mult).then_inc(sem["xu_ready"], raised("xu_ready"))
                else:
                    z0 = 2 * (i - 4)
                    taps([zt[:, c, :] for c in range(2)], [x0c[:, z0 + c, :] for c in range(2)],
                         [lambda tp, z=z: parc("hy_w", 3 * z + tp) for z in (z0, z0 + 1)], "z_out")
                if i == 0:
                    dve.wait_ge(sem["trig_in"], due("trig_in", 16))
                    for r in range(5):
                        row = q[:, r, LAT] if r < 4 else k[:, 0, LAT]
                        tmp = scf[:, 1024 + 512 * (r % 2):1536 + 512 * (r % 2)]
                        dve.wait_ge(sem["rot_mm"], due("rot_mm", r + 1))
                        dve.wait_ge(sem["qkv_out"], due("qkv_out", min(r + 1, 5)))
                        TT(row, row, trig[:, 0, :], ALU.mult).then_inc(sem["dve_order"], raised("dve_order"))
                        TT(tmp, ax[:, r % 4, :], trig[:, 1, :], ALU.mult).then_inc(sem["dve_order"], raised("dve_order"))
                        dve.wait_ge(sem["dve_order"], now("dve_order"))
                        TT(row, row, tmp, ALU.add).then_inc(sem["rot_out"], raised("rot_out"))
                else:
                    if i >= 2:
                        tpv(i - 2)
                    soft(i - 1)
            tpv(4)
            split(gF + 1)
            dve.wait_ge(sem["pads_at"], due("pads_at", 1))
            for n in range(10):
                dve.wait_ge(sem["filt_mm"], due("filt_mm", n + 1))
                dve.wait_ge(sem["win_in"], due("win_in", 16 * (n // 4 + 1)))
                TT(prod[:, n % 2, :], ax[:, n % 4, :], win[:, n % 4, :], ALU.mult).then_inc(sem["filt_out"], raised("filt_out"))
                if n % 2 == 0:
                    continue
                dve.wait_ge(sem["filt_out"], now("filt_out"))
                b = max(n // 2 - 1, 0)
                TT(sreg[:, b, :], prod[:, 0, :], prod[:, 1, :], ALU.add).then_inc(sem["gs_src" if n == 1 else "dve_order"], raised("gs_src" if n == 1 else "dve_order"))
                TT(dreg[:, :], prod[:, 0, :], prod[:, 1, :], ALU.subtract).then_inc(sem["gs_src"], raised("gs_src"))
                if n == 1:
                    lo(vlo[:, 0, :], sreg[:, 0, :], vhi[:, 0, :], "gs_hi", 1, "gs_ready")
                nn = n // 2 + 2
                v = GS_V[nn - 1]
                lo(vlo[:, v, :], dreg[:, :], vhi[:, v, :], "gs_hi", nn, "gs_ready")
                dve.wait_ge(sem["gs_ready"], now("gs_ready"))
            for n in range(4):
                a, b, op = ((0, 2, ALU.add), (1, 3, ALU.add), (0, 2, ALU.subtract), (1, 3, ALU.subtract))[n]
                TT(prod[:, n % 2, :], sreg[:, a, :], sreg[:, b, :], op).then_inc(sem["gs_src"], raised("gs_src"))
                lo(vlo[:, 2 + n, :], prod[:, n % 2, :], vhi[:, 2 + n, :], "gs_hi", 7 + n, "gs_ready")
                dve.wait_ge(sem["gs_ready"], now("gs_ready"))
            split(gF + 2)
            split(gF + 3)
            dve.wait_ge(sem["gsp_mm"], due("gsp_mm", 10))
            for b in range(NB):
                dve.wait_ge(sem["ut_mm"], due("ut_mm", b + 1))
                V.tensor_copy(ureg[:, b, :], ax[:, b % 4, :]).then_inc(sem["ut_out"], raised("ut_out"))
            dve.wait_ge(sem["ut_out"], now("ut_out"))
            for n in range(5):
                TS(ureg[:, n, :], ureg[:, n, :], 1.0, None, ALU.mult).then_inc(sem["us_src"], raised("us_src"))
            for n in range(5):
                v = US_V[n]
                lo(vlo[:, v, :], ureg[:, n, :], vhi[:, v, :], "us_hi", n + 1, "us_ready")
            for n in range(4):
                a, b, op = ((1, 3, ALU.add), (2, 4, ALU.add), (1, 3, ALU.subtract), (2, 4, ALU.subtract))[n]
                TT(ufold[:, n % 2, :], ureg[:, a, :], ureg[:, b, :], op).then_inc(sem["us_src"], raised("us_src"))
                lo(vlo[:, 2 + n, :], ufold[:, n % 2, :], vhi[:, 2 + n, :], "us_hi", 6 + n, "us_ready")
                dve.wait_ge(sem["us_ready"], now("us_ready"))
            for p_ in range(PAIRS):
                dve.wait_ge(sem["usp_out"], due("usp_out", 2 * p_ + 2))
                gr, gi = gsp[:, p_, 0, :], gsp[:, p_, 1, :]
                dve.wait_ge(sem["gsp_out"], due("gsp_out", 2 * p_ + 2))
                TT(prod[:, 0, :], us[:, 0, :], gr, ALU.mult).then_inc(sem["dve_order"], raised("dve_order"))
                TT(prod[:, 1, :], us[:, 1, :], gi, ALU.mult).then_inc(sem["dve_order"], raised("dve_order"))
                dve.wait_ge(sem["dve_order"], now("dve_order"))
                TT(us[:, 0, :], us[:, 0, :], gi, ALU.mult).then_inc(sem["dve_order"], raised("dve_order"))
                TT(us[:, 1, :], us[:, 1, :], gr, ALU.mult).then_inc(sem["dve_order"], raised("dve_order"))
                dve.wait_ge(sem["dve_order"], now("dve_order"))
                real = p_ < 2
                TT(us[:, 0, :], us[:, 0, :], us[:, 1, :], ALU.add).then_inc(sem["dve_order" if real else "y_src"], raised("dve_order" if real else "y_src"))
                if real:
                    dve.wait_ge(sem["dve_order"], now("dve_order"))
                    V.tensor_copy(us[0:1, 0, :], prod[0:1, 1, :]).then_inc(sem["y_src"], raised("y_src"))
                dve.wait_ge(sem["y_src"], now("y_src"))
                TT(us[:, 1, :], prod[:, 0, :], prod[:, 1, :], ALU.subtract).then_inc(sem["dve_order" if real else "y_src"], raised("dve_order" if real else "y_src"))
                if real:
                    dve.wait_ge(sem["dve_order"], now("dve_order"))
                    V.tensor_copy(us[0:1, 1, :], prod[0:1, 0, :]).then_inc(sem["y_src"], raised("y_src"))
                for o in range(2):
                    ys = Y_SLOT[p_]
                    lo(ylo[:, ys, 1 - o, :], us[:, o, :], yhi[:, ys, 1 - o, :], "y_hi", 2 * p_ + o + 1, "y_ready")
                if p_ == 2:
                    dve.wait_ge(sem["cinv_mm"], due("cinv_mm", 1))
                    for j in range(NHY):
                        STT(xu[:, j, CTX], xu[:, j, CTX], parc("hy_bias", j), ax[:, 0, P * j:P * (j + 1)],
                               ALU.mult, ALU.add).then_inc(sem["cinv_out" if j == 3 else "dve_order"], raised("cinv_out" if j == 3 else "dve_order"))
                    dve.wait_ge(sem["cinv_out"], now("cinv_out"))
                    TT(xu[:, :, CTX], xu[:, :, CTX], x0c[:, :, CTX], ALU.mult).then_inc(sem["dve_order"], raised("dve_order"))
                    split(gF + 4)
                if p_ == 3:
                    split(gF + 5)
            split(gF + 6)
            h_all(1, SH1, SC1)
            dve.wait_ge(sem["linv_mm"], due("linv_mm", 4))
            for j in range(NHY):
                STT(xu[:, j, LAT], xu[:, j, LAT], parc("hy_bias", j), ax[:, j, :], ALU.mult, ALU.add).then_inc(sem["dve_order"], raised("dve_order"))
            dve.wait_ge(sem["dve_order"], now("dve_order"))
            for j in range(NHY):
                TT(xu[:, j, LAT], xu[:, j, LAT], x0c[:, j, LAT], ALU.mult).then_inc(sem["hy_src"], raised("hy_src"))
            for j in range(NHY):
                lo(hyl[:, j, :], xu[:, j, :], hyh[:, j, :], "hy_hi", j + 1, "hy_ready")
            for m in range(KD):
                g = at_g("gate", m)
                split(g + 1)
                split(g + 2)
                for c in range(2):
                    dve.wait_ge(sem["gate_out"], due("gate_out", 2 * m + c + 1))
                    dve.wait_ge(sem["proj_mm"], due("proj_mm", 2 * m + c + 1))
                    TT(two(gates[:, c, :]), two(gates[:, c, :]), pair(TILES.index((g + 1, c))), ALU.mult).then_inc(sem["proj_out"], raised("proj_out"))
                dve.wait_ge(sem["proj_out"], now("proj_out"))
                TT(gates[:, 0, :], gates[:, 0, :], gates[:, 1, :], ALU.add).then_inc(sem["m_src"], raised("m_src"))
                lo(mlo(m), gates[:, 0, :], mhi[:, m, :], "m_hi", m + 1, "m_ready")
            for i in range(4):
                g = at_g("out", i)
                split(g + 1)
                for c in range(2):
                    m = 2 * i + c
                    dve.wait_ge(sem["out_mm"], due("out_mm", m + 1))
                    dve.wait_ge(sem["x_scaled"], due("x_scaled", m + 1))
                    residual(m, TILES.index((g, c)), G1, "out_out")
                    if m:
                        sum2(m - 1, m)
            sum2(KD - 1, KD)
            for w in range(2):
                dve.wait_ge(sem["stat_mm"], due("stat_mm", w + 1))
                TS(small[:, 76:86], ax[:, 3, 0:2 * NB], 1 / D_MODEL, None, ALU.mult).then_inc(sem["dve_order"], raised("dve_order"))
                dve.wait_ge(sem["dve_order"], now("dve_order"))
                TT(small[:, 66:71], small[:, 76:81], small[:, 76:81], ALU.mult).then_inc(sem["dve_order"], raised("dve_order"))
                dve.wait_ge(sem["dve_order"], now("dve_order"))
                TT(small[:, 66:71], small[:, 81:86], small[:, 66:71], ALU.subtract).then_inc(sem["dve_order"], raised("dve_order"))
                dve.wait_ge(sem["dve_order"], now("dve_order"))
                TS(small[:, 66:71], small[:, 66:71], 0.0, LN_EPS, ALU.max, ALU.add).then_inc(sem["ln_var"], raised("ln_var"))
                dve.wait_ge(sem["ln_sqrt"], due("ln_sqrt", w + 1))
                V.reciprocal(small[:, 86:91], small[:, 71:76]).then_inc(sem["dve_order"], raised("dve_order"))
                dve.wait_ge(sem["dve_order"], now("dve_order"))
                STT(small[:, 91:96], small[:, 76:81], -1.0, small[:, 86:91], ALU.mult, ALU.mult).then_inc(sem["dve_order"], raised("dve_order"))
                dve.wait_ge(sem["dve_order"], now("dve_order"))
                for i in range(2 * NB):
                    TS(diag[:, i, :], ident[:, :], small[:, 86 + i:87 + i], None, ALU.mult).then_inc(sem["diag_out" if i == 2 * NB - 1 else "dve_order"], raised("diag_out" if i == 2 * NB - 1 else "dve_order"))
                dve.wait_ge(sem["bc_mm"], due("bc_mm", w + 1))
                for i in range(KD + 2 * (w == 0)):
                    if i < KD:
                        for n in range(2):
                            if n:
                                dve.wait_ge(sem["dve_order"], now("dve_order"))
                            op = (ALU.mult, ALU.add)[n]
                            TT(x[:, i, CTX], x[:, i, CTX], ax[:, 2, P * n:P * (n + 1)], op).then_inc(sem["dve_order"], raised("dve_order"))
                            TT(x[:, i, LAT], x[:, i, LAT], ax[:, n, :], op).then_inc(sem["ln_norm" if n else "dve_order"], raised("ln_norm" if n else "dve_order"))
                    if w == 0 and 1 <= i <= KD:
                        dve.wait_ge(sem["ln_x"], due("ln_x", i))
                        h_src(2, i - 1, SH2, SC2)
                    if w == 0 and i >= 2:
                        h_lo(2, i - 2)
                if w:
                    break
                for hf in range(2):
                    for j in range(FH):
                        jj = FH * hf + j
                        g = at_g("up", jj)
                        split(g + 1)
                        sl = jj % 2
                        dve.wait_ge(sem["up_acc"], due("up_acc", jj + 1))
                        taps([gz[:, sl, :]], [ga[:, sl, :]], [lambda tp: parc("ff_w", 3 * jj + tp)], "up_taps")
                        dve.wait_ge(sem["up_gelu"], due("up_gelu", jj + 1))
                        dve.wait_ge(sem["up_mm"], due("up_mm", 2 * jj + 2))
                        TT(two(ga[:, sl, :]), two(ga[:, sl, :]), pair(TILES.index((g, 1))), ALU.mult).then_inc(sem["up_out"], raised("up_out"))
                        lo(actl[:, j, :], ga[:, sl, :], acth[:, j, :], "act_hi", jj + 1, "act_ready")
                        if L + 1 < DEPTH:
                            if jj == 0:
                                dve.wait_ge(sem["cond_rows"], L + 1)
                            ada_t(ADA_FFN[g])
                    for m in range(KD):
                        g = at_g("down", KD * hf + m)
                        if g + 1 < NG:
                            split(g + 1)
                        dve.wait_ge(sem["down_mm"], due("down_mm", KD * hf + m + 1))
                        dve.wait_ge(sem["x_scaled"], due("x_scaled", KD + m + 1))
                        residual(m, TILES.index((g, 0)), G2, "down_out")
                        if hf and m:
                            sum2(m - 1, KD + m)
                        if L + 1 < DEPTH and g in ADA_FFN:
                            ada_t(ADA_FFN[g])
                sum2(KD - 1, 2 * KD)
            lane.end()
        for b in range(NB):
            if b >= 2:
                dve.wait_ge(sem["y_dma"], 16 * (b - 1))
            dve.wait_ge(sem["y_mm"], b + 1)
            V.tensor_copy(yout[:, b % 2, :].rearrange("p (a c) -> p a c", a=2),
                          ax[:, 2 * (b % 2):2 * (b % 2) + 2, :]).then_inc(sem["y_out"], 1)

    @block.gpsimd
    def _(pool):
        lane = Counts("pool_order")
        due, raised, now = lane.due, lane.raised, lane.now
        G = nc.gpsimd
        G.memset(x[:, :, :], 0.0).then_inc(sem["x_zero"], 1)

        def zero_pads(bufs, event):
            n = 3 * len(bufs)
            for b in bufs:
                for a, e in ((0, 1), (C0 + SEQ, L0), (ROW - 1, ROW)):
                    n -= 1
                    G.memset(b[:, :, a:e], 0.0).then_inc(sem[event if n == 0 else "pool_order"], raised(event if n == 0 else "pool_order"))

        def scaled(h, first):
            for d in range(KD):
                pool.wait_ge(sem["h_ready"], due("h_ready", h * KD + d + 1))
                G.tensor_scalar(x[:, d, :], x[:, d, :], ALPHA, None, ALU.mult).then_inc(sem["x_scaled"], raised("x_scaled"))

        def sum1(event, first):
            for m in range(KD):
                pool.wait_ge(sem[event], due(event, first + m + 1))
                if m == 0:
                    G.tensor_copy(sums[:, 0, :], x[:, 0, :]).then_inc(sem["sum1_out"], raised("sum1_out"))
                else:
                    pool.wait_ge(sem["sum1_out"], now("sum1_out"))
                    G.tensor_tensor(sums[:, 0, :], sums[:, 0, :], x[:, m, :], ALU.add).then_inc(sem["sum1_out"], raised("sum1_out"))

        for L in range(DEPTH):
            lane.start(L)
            if L == 0:
                pool.wait_ge(sem["mlp_arg"], 6)
            pool.wait_ge(sem["m_ready"], due("m_ready", 0))
            pool.wait_ge(sem["h_ready"], due("h_ready", 0))
            zero_pads([hsrc], "pads_h")
            pool.wait_ge(sem["ln_x"], due("ln_x", 0))
            pool.dma_start(par[:, 0:NPAR], A["par"][L]).then_inc(sem["params_in"], 16)
            pool.wait_ge(sem["h_ready"], due("h_ready", KD))
            pool.dma_start(trig[:, :, :], A["trig"]).then_inc(sem["trig_in"], 16)
            pool.wait_ge(sem["qkv_out"], due("qkv_out", 4))
            zero_pads([f32(ath[:, :, :]), f32(atl[:, :, :])], "pads_at")
            pool.wait_ge(sem["vt_out"], due("vt_out", 4))
            pool.dma_start(A["out_k"][L], kout[:, :]).then_inc(sem["kv_dma"], 16)
            pool.dma_start(A["out_v"][L], vtok[:, 0, :]).then_inc(sem["kv_dma"], 16)
            pool.wait_ge(sem["kv_dma"], 32 * (L + 1))
            pool.wait_ge(sem["pv_mm"], due("pv_mm", 40))
            pool.wait_ge(sem["ot_mm"], due("ot_mm", 5))
            pool.dma_start(w3[:, :], A["w3"][L]).then_inc(sem["w3_in"], 16)
            for n, (a, b) in enumerate(((0, 4), (4, 8), (8, 10))):
                if n:
                    pool.wait_ge(sem["filt_out"], due("filt_out", a))
                pool.dma_start(win[:, 0:b - a, :], A["window"][:, a:b, :]).then_inc(sem["win_in"], 16)
                pool.wait_ge(sem["win_in"], 48 * L + 16 * (n + 1))
            pool.wait_ge(sem["y_ready"], due("y_ready", 10))
            pool.wait_ge(sem["pads_at"], now("pads_at"))
            zero_pads([hsrc], "pads_h")
            scaled(1, 0)
            pool.wait_ge(sem["m_ready"], due("m_ready", KD))
            pool.wait_ge(sem["x_scaled"], now("x_scaled"))
            zero_pads([hsrc], "pads_h")
            sum1("out_out", 0)
            if L + 1 < DEPTH:
                pool.wait_ge(sem["bc_mm"], due("bc_mm", 1))
                pool.dma_start(crow[:, :, :], A["cond_rows"]).then_inc(sem["cond_rows_in"], 16)
            scaled(2, KD)
            sum1("down_out", KD)
            lane.end()

    st.close()


def _dft_constants():
    def forward(freqs, n_in, length):
        ang = 2 * np.pi * np.outer(np.arange(n_in), freqs) / length
        return np.cos(ang), -np.sin(ang)

    def back(freqs, n_out, length):
        ang = 2 * np.pi * np.outer(freqs, np.arange(n_out)) / length
        return 2 * np.cos(ang) / length, -2 * np.sin(ang) / length

    f0, i0, i1 = [], [], []
    N, NC = 2 * DEC_SEQ, 2 * SEQ
    kk = np.arange(SEQ // 2)
    zero = np.zeros((SEQ, SEQ // 2))
    ev, od = forward(2 * kk, SEQ, NC), forward(2 * kk + 1, SEQ, NC)
    ny = np.cos(np.pi * np.arange(SEQ))
    evi = ev[1].copy()
    evi[:, 0] = ny
    ctx = [np.hstack([ev[0], zero]), np.hstack([zero, od[0]]), np.hstack([evi, zero]), np.hstack([zero, od[1]])]
    br, bi = back(np.concatenate([2 * kk, 2 * kk + 1]), SEQ, NC)
    br[0] /= 2
    bi[0] = np.cos(np.pi * np.arange(SEQ)) / NC
    cinv = [br, bi]
    k4 = np.arange(P)
    lat = []
    for add in (0, 2):
        re, im = forward(4 * k4 + add, DEC_SEQ // 2, N)
        if add == 0:
            im = im.copy()
            im[:, 0] = np.cos(np.pi * np.arange(DEC_SEQ // 2))
        lat += [re[:P], re[P:], im[:P], im[P:]]
        br, bi = back(4 * k4 + add, DEC_SEQ, N)
        if add == 0:
            br[0] /= 2
            bi[0] = np.cos(np.pi * np.arange(DEC_SEQ)) / N
        i0 += [br, bi]
    f0 = ctx + lat + cinv
    f1 = []
    for o in range(2):
        fr = 2 * (P * o + np.arange(P)) + 1
        re, im = forward(fr, DEC_SEQ, N)
        f1 += [m[P * b:P * (b + 1)] for m in (re, im) for b in range(4)]
        i1 += list(back(fr, DEC_SEQ, N))
    cat = lambda xs: np.ascontiguousarray(np.hstack(xs).astype(np.float32))
    return {"F0": cat(f0), "F1": cat(f1), "I0": cat(i0), "I1": cat(i1)}


def _shape_constants():
    out = _dft_constants()
    out["ident"] = np.eye(P, dtype=np.float32)
    out["ones"] = np.ones((P, P), np.float32)
    r = np.zeros((P, P), np.float32)
    for a in range(0, P, 32):
        for i in range(16):
            r[a + 16 + i, a + i] = -1.0
            r[a + i, a + 16 + i] = 1.0
    out["rot"] = r
    inv = 1.0 / (10000.0 ** (np.arange(0, 32, 2, dtype=np.float32) / np.float32(32)))
    pos = np.stack([np.repeat(np.arange(DEC_SEQ // 64), 64), np.tile(np.arange(64), DEC_SEQ // 64)])
    ang = pos.astype(np.float32)[:, None, :] * inv.astype(np.float32)[None, :, None]
    ang = np.tile(np.concatenate([ang, ang], axis=1).reshape(HD, DEC_SEQ), (2, 1))
    out["trig"] = np.ascontiguousarray(np.stack([np.cos(ang), np.sin(ang)], axis=1).astype(np.float32))
    i, j = np.indices((P, P))
    zero = np.zeros((P, P))
    prev, nxt = np.where(j >= i, 0, -1e30), np.where(j <= i, 0, -1e30)
    out["mask"] = np.hstack([zero, prev, zero, nxt, zero]).astype(np.float32)

    def times(L):
        t = np.linspace(0.0, 1.0, L, dtype=np.float32)
        w = (2.0 * math.pi * np.arange(L, dtype=np.float32) / L).astype(np.float32)
        f = np.linspace(1e-4, 15, 16, dtype=np.float32)
        z = w[:, None] * f[None, :]
        feats = np.concatenate([t[:, None], np.cos(z), -np.sin(z)], axis=1).astype(np.float32)
        rates = np.abs(np.linspace(math.log(1e-2) / 1.5, math.log(1e-2) / 0.3, HY_W, dtype=np.float32))
        window = np.exp(-t[:, None] * rates[None, :]).astype(np.float32)
        back = (L - np.arange(L)) % L
        wback = window[back].copy()
        wback[0] = 0.0
        return feats, feats[back], window, wback

    fc, fcb, wc, wcb = times(SEQ)
    fl, flb, wl, wlb = times(DEC_SEQ)
    out["feat"] = np.ascontiguousarray(np.concatenate([fc, fcb, fl, flb]).T)
    blocks = [wc, wcb]
    for b in range(4):
        blocks += [wl[P * b:P * (b + 1)], wlb[P * b:P * (b + 1)]]
    out["window"] = np.ascontiguousarray(np.stack(blocks, axis=1))
    return out


def _layouts(i):
    out = {}
    D = DEPTH

    def chunks(w, tiles):
        d, kk, n = w.shape
        w = w.reshape(d, kk // P, P, n // (P * tiles), tiles, P)
        return np.ascontiguousarray(w.transpose(0, 3, 2, 4, 1, 5)).reshape(d, n // (P * tiles), P, -1)

    w_in = np.asarray(i["w_in"])
    qw, rest = w_in[..., :512], w_in[..., 512:]
    heads = [g * 4 + j for j in range(4) for g in range(2)]
    qw = qw.reshape(D, D_MODEL, NH, HD)[:, :, heads].reshape(D, D_MODEL, 512)
    out["w_q"] = chunks(qw, 2)
    out["w_k"], out["w_v"] = chunks(rest[..., 0:P], 1), chunks(rest[..., P:2 * P], 1)
    z = rest[..., 2 * P:2 * P + 3 * HY_W].reshape(D, D_MODEL, 12, P)
    order = [t for n in range(4) for t in (4 + n, 8 + n)] + [0, 1, 2, 3]
    out["w_z"] = chunks(z[:, :, order].reshape(D, D_MODEL, 12 * P), 2)
    ga = rest[..., 2 * P + 3 * HY_W:].reshape(D, D_MODEL, 2, KD, P)
    out["w_gate"] = chunks(ga.transpose(0, 1, 3, 2, 4).reshape(D, D_MODEL, 16 * P), 2)
    pa = np.asarray(i["w_pa"]).reshape(D, NH, HD, D_MODEL)[:, heads].reshape(D, 512, D_MODEL)
    out["w_proj"] = chunks(np.concatenate([pa, np.asarray(i["w_pb"])], axis=1), 1)
    out["w_out"] = chunks(np.asarray(i["w_out"]), 2)
    up = np.asarray(i["w_up"]).reshape(D, D_MODEL, 2, NFF, P).transpose(0, 1, 3, 2, 4)
    out["w_up"] = chunks(up.reshape(D, D_MODEL, 2 * D_FF), 2)
    down = np.asarray(i["w_down"]).reshape(D, 2, D_FF // 2, D_MODEL)
    out["w_down"] = np.ascontiguousarray(np.concatenate([chunks(down[:, 0], 1), chunks(down[:, 1], 1)], axis=1))
    w_ada = np.asarray(i["w_ada"])
    out["ada"] = chunks(w_ada, 2)[0]
    w_t = w_ada[1:].transpose(0, 2, 1).reshape(D - 1, ADA_STEPS, 2, P, D_MODEL)
    out["ada_t"] = np.ascontiguousarray(w_t.transpose(0, 1, 3, 2, 4)).reshape(D - 1, ADA_STEPS, P, CHUNK)
    col = lambda v: np.asarray(v).reshape(D, -1, P).transpose(0, 2, 1)
    tap = lambda w: np.asarray(w).reshape(D, 3, -1, P).transpose(0, 3, 2, 1).reshape(D, P, -1)
    sink = np.broadcast_to(np.asarray(i["attn_sink"])[:, None, heads], (D, P, NH))
    ck = np.asarray(i["cache_k"])[0].reshape(D, PAST, P)
    cv = np.asarray(i["cache_v"])[0].reshape(D, PAST, P)
    out["par"] = np.ascontiguousarray(np.concatenate([
        col(i["b_ada"]), tap(i["hy_conv_w"]), col(i["hy_conv_b"]), col(i["hy_bias"]), col(i["ln1_g"]),
        col(i["ln1_b"]), col(i["ln2_g"]), col(i["ln2_b"]), tap(i["ffn_conv_w"]), col(i["ffn_conv_b"]),
        sink, ck, cv], axis=2))
    c2 = np.stack([np.asarray(i["c_ctx"]), np.asarray(i["c"])[0]], axis=-1)
    out["cond_rows"] = np.ascontiguousarray(np.broadcast_to(c2.T, (P, 2, D_MODEL)))
    out["cond"] = np.ascontiguousarray(c2.reshape(KD, P, 2).transpose(1, 0, 2))
    hid = np.asarray(i["filt_w2"]).shape[1]
    out["w1"] = np.ascontiguousarray(np.concatenate(list(np.asarray(i["filt_w1"])), axis=1))
    w2 = np.zeros((P, P), np.float32)
    w3 = np.zeros((D, P, 2 * HY_W), np.float32)
    for l in range(D):
        w2[hid * l:hid * (l + 1), hid * l:hid * (l + 1)] = np.asarray(i["filt_w2"])[l]
        w3[l, hid * l:hid * (l + 1)] = np.asarray(i["filt_w3"])[l]
    out["w2"], out["w3"] = w2, w3
    out["mlpv"] = np.ascontiguousarray(np.stack(
        [np.asarray(i[n]).reshape(-1) for n in ("filt_b1", "filt_freq1", "filt_b2", "filt_freq2")], axis=1))
    out["x_prompt"], out["x_sample"] = np.asarray(i["x_prompt"]), np.asarray(i["x_sample"])
    return out


def kernel(**inputs):
    import concourse.bacc as bacc
    from concourse.bass_utils import run_bass_kernel_spmd

    nc = bacc.Bacc("TRN2", target_bir_lowering=False, num_devices=1)
    arrays = {**_layouts(inputs), **_shape_constants()}
    A = {n: nc.dram_tensor("in_" + n, a.shape, mybir.dt.from_np(a.dtype), kind="ExternalInput").ap()
         for n, a in arrays.items()}
    outs = {"y_prompt": (1, SEQ, D_MODEL), "y_sample": (1, DEC_SEQ, D_MODEL),
            "out_k": (DEPTH, SEQ, NKV * HD), "out_v": (DEPTH, SEQ, NKV * HD)}
    for n, s in outs.items():
        A[n] = nc.dram_tensor("res_" + n, s, F32, kind="ExternalOutput").ap()
    _program(nc, A)
    r = run_bass_kernel_spmd(nc, [{"in_" + n: a for n, a in arrays.items()}], core_ids=[0]).results[0]
    cache = (1, DEPTH, SEQ, NKV, HD)
    return (r["res_y_prompt"], r["res_y_sample"], r["res_out_k"].reshape(cache), r["res_out_v"].reshape(cache))
```

```python
import math
from contextlib import ExitStack

import numpy as np
import concourse.bass as bass
from concourse import mybir

F32 = mybir.dt.float32
F32R = mybir.dt.float32r
BF16 = mybir.dt.bfloat16
ACT = mybir.ActivationFunctionType
ALU = mybir.AluOpType

P = 128
D_MODEL, DEPTH = 1024, 2
SEQ, DEC_SEQ, PAST = 128, 512, 128
HD, NH, NKV = 64, 8, 2
HY_W, D_FF = 512, 2816
ALPHA = (2 * DEPTH) ** 0.25
LN_EPS = 1e-5
KD = D_MODEL // P
NB = (SEQ + DEC_SEQ) // P
ROW = SEQ + DEC_SEQ + 4
HALF = ROW // 2
C0, L0 = 1, SEQ + 3
CTX, LAT = slice(C0, C0 + SEQ), slice(L0, L0 + DEC_SEQ)
NFF = D_FF // P
FH = NFF // 2
NHY = HY_W // P

CHUNK = 2048
ADA_STEPS = 6 * D_MODEL // 256
ADA_FIRST = 2 * D_MODEL // 256
ADA_GROUP = D_MODEL // 256
DOWN_W = FH * P
F0_BLOCKS, F1_BLOCKS = 14, 16
GEMM = ([("q", 0), ("q", 1), ("k", 0), ("v", 0)] + [("z", i) for i in range(6)]
        + [("F", 1), ("F", 0), ("I", 0), ("F", 1), ("I", 1)]
        + [x for m in range(KD) for x in (("gate", m), ("proj", m))]
        + [("out", i) for i in range(4)]
        + [("up", j) for j in range(FH)] + [("down", m) for m in range(KD)]
        + [("up", FH + j) for j in range(FH)] + [("down", KD + m) for m in range(KD)])
NG = len(GEMM)
WIDTH = {"q": 2048, "k": 1024, "v": 1024, "z": 2048, "gate": 2048, "proj": 1024, "out": 2048,
         "up": 2048, "down": DOWN_W}
WG = [g for g in range(NG) if GEMM[g][0] not in "FI"]


def width(g):
    kind, i = GEMM[g]
    if kind == "F":
        return (F0_BLOCKS, F1_BLOCKS)[i] * P
    return CHUNK if kind == "I" else WIDTH[kind]


def stream():
    order = [(0, "ada", s) for s in range(ADA_FIRST)]
    gf = at_g("F", 1)
    for layer in range(DEPTH):
        for g in range(NG):
            order.append((layer, "g", g))
            if layer == 0 and gf - 4 <= g < gf:
                first = ADA_FIRST + ADA_GROUP * (g - gf + 4)
                order += [(layer, "ada", s) for s in range(first, first + ADA_GROUP)]
            if layer + 1 < DEPTH and g - 1 in ADA_FFN:
                order.append((layer + 1, "ada", ADA_FFN[g - 1]))
    return order


def at_g(kind, i=0, nth=0):
    return [g for g in range(NG) if GEMM[g] == (kind, i)][nth]


ADA_FFN = {g: n for n, g in enumerate([g for g in range(at_g("up"), NG) if GEMM[g][0] == "up" or GEMM[g][1] < 2])}
assert len(ADA_FFN) == ADA_STEPS

PAR = {}
NPAR = 0
for _name, _n in (("b_ada", 48), ("hy_w", 36), ("hy_b", 12), ("hy_bias", 4), ("ln1_g", 8),
                  ("ln1_b", 8), ("ln2_g", 8), ("ln2_b", 8), ("ff_w", 66), ("ff_b", 22),
                  ("sink", 8), ("cache_k", 128), ("cache_v", 128)):
    PAR[_name] = NPAR
    NPAR += _n

FEAT = 33
NT = 2 * (SEQ + DEC_SEQ)
PAIRS = 5
SH1, SC1, G1, SH2, SC2, G2 = (8 * _i for _i in range(6))

KEYS = [[("own", 0, 1)], [("lat", 0, 2), ("ctx", 0, 1)], [("ctx", 0, 1), ("lat", 0, 3)],
        [("ctx", 0, 1), ("lat", 1, 3)], [("ctx", 0, 1), ("lat", 2, 2)]]
MASK_AT = [0, 2, 0, 0, 0]
TWO_PI_PARTS = (6.28125, 0.0019350051879882812, 3.0199159819120541e-07)
MAGIC = 12582912.0
KV_SPACE = 3 * HY_W

EVENTS = dict(
    params_in=16, trig_in=16, w3_in=16, win_in=16 * 4, mod_done=6, w_hi=NG, w_split=NG,
    h_src=2 * KD, h_hi=3 * KD, h_ready=3 * KD, x_scaled=2 * KD,
    qkv_mm=6, qkv_out=6, rot_mm=5, rot_out=5, vt_mm=2, vt_out=4,
    z_mm=12, z_raw=12, z_acc=12, z_out=12, xu_ready=4,
    qk_mm=40, qk_out=40, soft_m=5, exp_out=40,
    pt_mm=40, pt_act=20, pt_dve=20, pv_mm=40, osb_out=5, ot_mm=5, at_hi=5, at_lo=5,
    filt_mm=10, filt_out=10, gs_src=10, gs_hi=10, gs_ready=10, gsp_mm=10, gsp_out=10,
    ut_mm=5, ut_out=5, us_src=4, us_hi=9, us_ready=9, usp_mm=10, usp_out=10,
    y_src=10, y_hi=10, y_ready=10, cinv_mm=1, cinv_out=1, linv_mm=4, hy_src=4, hy_hi=4, hy_ready=4,
    gate_mm=16, gate_out=16, proj_mm=16, proj_out=16, m_src=8, m_hi=8, m_ready=8,
    out_mm=8, out_out=8, up_mm=44, up_raw=22, up_acc=22, up_taps=22, up_gelu=22, up_out=22,
    act_hi=22, act_ready=22, down_mm=16, down_out=16, sq_out=16, sum1_out=16, sum2_out=16,
    stat_mm=2, ln_var=2, ln_sqrt=2, diag_out=4 * NB, bc_mm=4, ln_scaled=16, ln_shift=4, ln_norm=16, ln_x=16,
    pads_h=3, pads_at=1, kv_dma=32, dve_order=1, act_order=1, pool_order=1,
)
CREDIT = dict(w_split=2, down_mm=2, ln_x=1, m_ready=1, h_ready=1)


class Counts:

    def __init__(self, order):
        self.order = order
        self.layer, self.n = 0, {}

    def start(self, layer):
        self.layer = layer

    def raised(self, event):
        self.n[event] = self.n.get(event, 0) + 1
        return 1

    def slot_of(self, g):
        return (self.layer * NG + g) % 2

    def due(self, event, n):
        return self.layer * EVENTS[event] + CREDIT.get(event, 0) + n

    def now(self, event):
        return CREDIT.get(event, 0) + self.n[event]

    def end(self):
        for e, n in self.n.items():
            assert e == self.order or n == DEPTH * EVENTS[e], (e, n, EVENTS[e])


def _program(nc, A):
    st = ExitStack()
    sem = {n: st.enter_context(nc.semaphore(n)) for n in EVENTS}
    for n in ("raw0", "raw1", "ada_mm", "row_first", "row_act", "row_dve", "col_mm", "ada_t",
              "cond_rows_in", "cond_rows", "b_next_in", "cond_in", "x_in", "consts_in", "x_zero",
              "cond_ready", "x_tr", "x_row", "mlp_mm", "mlp_arg", "mlp_sin", "mlp_order", "mask_done",
              "y_mm", "y_out", "y_out_act", "y_dma"):
        sem[n] = st.enter_context(nc.semaphore(n))

    def sb(name, shape, dt=F32, where=st):
        return where.enter_context(nc.sbuf_tensor(name, shape, dt))

    x = sb("x", [P, KD, ROW])
    raw = [sb(f"w_raw{i}", [P, CHUNK]) for i in range(2)]
    whi = [sb(f"w_hi{i}", [P, CHUNK], F32R) for i in range(2)]
    wlo = [sb(f"w_lo{i}", [P, CHUNK], F32R) for i in range(2)]
    par = sb("par", [P, -(-NPAR // 16) * 16])
    ident = sb("ident", [P, P])
    rot = sb("rot", [P, P])
    ones = sb("ones", [P, P])
    mask = sb("mask", [P, 5 * P], BF16)
    h2T = sb("h2T", [P, NT])
    cs = sb("cs", [P, KD, 2])
    mod = sb("mod", [P, 48, 2])
    small = sb("small", [P, 96])

    with ExitStack() as s:
        trig = sb("trig", [P, 2, DEC_SEQ], F32, s)
    with ExitStack() as s:
        prod = sb("prod", [P, 2, HY_W], F32, s)
    with ExitStack() as s:
        hsrc = sb("h_src_rows", [P, 2, ROW], F32, s)
    with ExitStack() as s:
        sb("trig_space", [P, 2 * DEC_SEQ], F32, s)
        rows = sb("mod_rows", [P, 2, P], F32, s)
    gates = sb("gates", [P, 2, ROW])
    with ExitStack() as s:
        rows0 = sb("mod_rows_first", [P, 4 * ADA_GROUP, P], F32, s)
        xin = sb("x_in", [P, NB, D_MODEL], F32, s)
        feat = sb("feat", [FEAT, NT], F32, s)
        mask_in = sb("mask_in", [P, 5 * P], F32, s)
        w1 = sb("w1", [FEAT, P], F32, s)
        w2 = sb("w2", [P, P], F32, s)
        h1T = sb("h1T", [P, NT], F32, s)
    with ExitStack() as s:
        yout = sb("y_rows", [P, NB, D_MODEL], F32, s)
    with ExitStack() as s:
        vhi = sb("v_hi", [P, 10, HY_W], F32R, s)
        vlo = sb("v_lo", [P, 10, HY_W], F32R, s)
    hhi = sb("h_hi", [P, KD, ROW], F32R)
    hlo = sb("h_lo", [P, KD, ROW], F32R)
    with ExitStack() as s:
        with ExitStack() as s2:
            q = sb("q", [P, 4, ROW], F32, s2)
        ath = sb("attn_hi", [P, 4, ROW], F32R, s)
        with ExitStack() as s2:
            k = sb("k", [P, 1, ROW], F32, s2)
            vtok = sb("v_tok", [P, NB, P], F32, s2)
        with ExitStack() as s2:
            send = sb("filter_sums_end", [P, 2, HY_W], F32, s2)
            dreg = sb("d_block", [P, HY_W], F32, s2)
        with ExitStack() as s2:
            us = sb("u_spec", [P, 2, HY_W], F32, s2)
            uctx = sb("u_context", [P, HY_W], F32, s2)
        sb("k_v_space", [P, KV_SPACE], F32, s)
        atl = sb("attn_lo", [P, 4, ROW], F32R, s)
        with ExitStack() as s2:
            mlpv = sb("mlp_vec", [P, 4], F32, s2)
            turns2 = sb("sine_turns", [P, HY_W], F32, s2)
        x0c = sb("x0c", [P, NHY, ROW], F32, s)
        xu = sb("xu", [P, NHY, ROW], F32, s)
        with ExitStack() as s2:
            sc = sb("scores", [P, NH, 4 * P], F32, s2)
            pt = sb("p_t", [P, 2, 4 * P], F32, s2)
            osb = sb("o_sb", [P, 4 * P], F32, s2)
            kcT = sb("kcT", [P, P], F32, s2)
            kout = sb("k_out", [P, P], F32, s2)
            zt = sb("z_rows", [P, 2, ROW], F32, s2)
            ca = sb("z_acc", [P, 2, ROW], F32, s2)
            w3 = sb("w3", [P, 2 * HY_W], F32, s2)
        with ExitStack() as s2:
            hyh = sb("hy_hi", [P, NHY, ROW], F32R, s2)
            hyl = sb("hy_lo", [P, NHY, ROW], F32R, s2)
        with ExitStack() as s2:
            gsp = sb("g_spec", [P, PAIRS, 2, HY_W], F32, s2)
            with ExitStack() as s3:
                filt = sb("filter_blocks", [P, 6, HY_W], F32, s3)
            with ExitStack() as s3:
                ureg = sb("u_blocks", [P, 4, HY_W], F32, s3)
                ufold = sb("u_fold", [P, 4, HY_W], F32, s3)
            yhi = sb("y_hi", [P, 2, 2, HY_W], F32R, s2)
            ylo = sb("y_lo", [P, 2, 2, HY_W], F32R, s2)
    with ExitStack() as s:
        sb("attn_space", [P, 4 * ROW], F32, s)
        with ExitStack() as s2:
            mlb = sb("merged_lo_end", [P, 2, ROW], F32R, s2)
        sb("k_v_space2", [P, KV_SPACE], F32, s)
        sb("attn_lo_space", [P, 4 * ROW], F32, s)
        mhi = sb("merged_hi", [P, KD, ROW], F32R, s)
        sb("hy_space", [P, 8 * ROW], F32, s)
        mla = sb("merged_lo", [P, KD - 2, ROW], F32R, s)
    with ExitStack() as s:
        sums = sb("sums", [P, 2, ROW], F32, s)
        sq = sb("squares", [P, 2, ROW], F32, s)
        acth = sb("act_hi", [P, FH, ROW], F32R, s)
        actl = sb("act_lo", [P, FH, ROW], F32R, s)
        gz = sb("gate_rows", [P, 2, ROW], F32, s)
        ga = sb("gate_acc", [P, 2, ROW], F32, s)
        with ExitStack() as s2:
            crow = sb("cond_by_row", [P, 2, D_MODEL], F32, s2)
        diag = sb("diag", [P, 2 * NB, P], F32, s)

    ssum = [filt[:, 0, :], filt[:, 1, :], send[:, 0, :], send[:, 1, :]]

    def mlo(d):
        return mla[:, d, :] if d < KD - 2 else mlb[:, d - KD + 2, :]

    gp = st.enter_context(nc.psum_tensor("gemm_psum", [P, 4, 512], F32))
    ax = st.enter_context(nc.psum_tensor("aux_psum", [P, 4, 512], F32))

    def y_banks(b):
        return (ax, gp)[b // 2 % 2][:, 2 * (b % 2):2 * (b % 2) + 2, :]

    def pair(i):
        return gp[:, 2 * (i % 2):2 * (i % 2) + 2, 0:HALF]

    mlp_bank = lambda lay, n: ax[:, (n + 1) % 3, :] if lay else (gp[:, 2, :], gp[:, 3, :], ax[:, 0, :])[n]
    ADA_AT = 384

    def two(row):
        return row.rearrange("p (a b) -> p a b", a=2)

    def tok(b):
        at = C0 if b == 0 else L0 + P * (b - 1)
        return slice(at, at + P)

    scf = sc[:, :, :].rearrange("p a b -> p (a b)")
    vrow = scf[:, 0:ROW]
    parc = lambda name, i: par[:, PAR[name] + i:PAR[name] + i + 1]
    cache_k = par[:, PAR["cache_k"]:PAR["cache_k"] + P]
    cache_v = par[:, PAR["cache_v"]:PAR["cache_v"] + P]
    f32 = lambda ap: ap.bitcast(F32)

    TILES, last_read, n_of = [], [], {}
    for g, (kind, i) in enumerate(GEMM):
        for c in range({"F": 0, "I": 0, "k": 1, "v": 1, "down": 1}.get(kind, 2)):
            TILES.append((g, c))
            n = n_of[kind] = n_of.get(kind, 0) + 1
            last_read.append({
                "q": ("qkv_out", n), "k": ("qkv_out", 5), "v": ("qkv_out", 6), "z": ("z_acc", n),
                "gate": ("gate_out", n), "proj": ("proj_out", n), "out": ("out_out", n),
                "up": (("up_acc", (n + 1) // 2), ("up_out", n // 2))[c],
                "down": ("down_out", n)}[kind])
    n_of, chunk_done = {}, []
    for kind, i in GEMM:
        if kind in "FI":
            chunk_done.append(None)
            continue
        ev = "qkv_mm" if kind in "qkv" else kind + "_mm"
        n_of[ev] = n_of.get(ev, 0) + {"k": 1, "v": 1, "down": 1}.get(kind, 2)
        chunk_done.append((ev, n_of[ev]))
    gF = at_g("F", 1)
    STREAM = stream()
    STEP = {item: n for n, item in enumerate(STREAM)}
    chunk_done[gF:gF + 5] = [("gsp_mm", 4), ("cinv_mm", 1), ("linv_mm", 2), ("usp_mm", 10), ("linv_mm", 4)]
    G_V = [(0, 1), (2, 3), (4, 5), (6, 7, 8, 9), (6, 7, 8, 9)]
    U_V = [(0, 0)] + G_V[1:]
    GSP_PAIRS = [3, 4, 0, 1, 2]
    Y_SLOT = [0, 1, 0, 1, 0]
    GS_V = [0, 1, 6, 7, 8, 9, 2, 3, 4, 5]
    US_V = [6, 7, 8, 9, 0, 2, 3, 4, 5]
    key_blocks = [[(kd, f + i) for kd, f, m in ks for i in range(m)] for ks in KEYS]
    mm, tr = nc.tensor.matmul, nc.tensor.transpose
    block = st.enter_context(nc.Block())

    @block.sync
    def _(sp):
        lane = Counts(None)
        due = lane.due
        sp.dma_start(cs[:, :, :], A["cond"]).then_inc(sem["cond_in"], 16)
        for n, (L, what, i) in enumerate(STREAM):
            lane.start(L)
            if n == 2:
                sp.dma_start(ident[:, :], A["ident"]).then_inc(sem["x_in"], 16)
                sp.dma_start(xin[:, 0, :], A["x_prompt"][0]).then_inc(sem["x_in"], 16)
                sp.dma_start(xin[:, 1:NB, :], A["x_sample"][0].rearrange("(b p) d -> p b d", p=P))\
                    .then_inc(sem["x_in"], 16)
                for dst, src in ((feat, "feat"), (w1, "w1"), (w2, "w2"), (mlpv, "mlpv"), (rot, "rot"),
                                 (ones, "ones"), (mask_in, "mask")):
                    sp.dma_start(dst[:, :], A[src]).then_inc(sem["consts_in"], 16)
            if n >= 2:
                before = STREAM[n - 2]
                if before[1] == "ada" and before[0] == 0:
                    sp.wait_ge(sem["ada_mm"], 2 * (before[2] + 1))
                elif before[1] == "ada":
                    sp.wait_ge(sem["ada_t"], 4 * (ADA_STEPS * (before[0] - 1) + before[2] + 1))
                else:
                    sp.wait_ge(sem["w_split"], NG * before[0] + CREDIT["w_split"] + before[2] + 1)
            if what == "ada":
                src, w = A["ada"][i] if L == 0 else A["ada_t"][L - 1, i], CHUNK
            elif GEMM[i][0] in "FI":
                src, w = A["".join(map(str, GEMM[i]))], width(i)
            else:
                src, w = A["w_" + GEMM[i][0]][L, GEMM[i][1]], width(i)
            sp.dma_start(raw[n % 2][:, 0:w], src).then_inc(sem[f"raw{n % 2}"], 16)
        for b in range(NB):
            sp.wait_ge(sem["y_out"], b + 1)
            sp.wait_ge(sem["y_out_act"], b + 1)
            dst = A["y_prompt"][0] if b == 0 else A["y_sample"][0, P * (b - 1):P * b, :]
            sp.dma_start(dst, yout[:, b, :]).then_inc(sem["y_dma"], 16)
        sp.wait_ge(sem["y_dma"], 16 * NB)

    @block.tensor
    def _(pe):
        pe.sem_inc(sem["down_mm"], CREDIT["down_mm"])
        def ada(t):
            n = STEP[(0, "ada", t // 2)]
            pe.wait_ge(sem[f"raw{n % 2}"], 16 * (n // 2 + 1))
            for kk in range(KD):
                last = mm(gp[0:2, t % 2, ADA_AT:ADA_AT + P], cs[:, kk, :],
                          raw[n % 2][:, P * (KD * (t % 2) + kk):P * (KD * (t % 2) + kk + 1)],
                          start=kk == 0, stop=kk == KD - 1)
            last.then_inc(sem["ada_mm"], 1)

        pe.wait_ge(sem["cond_ready"], 1)
        for t in range(4):
            if t >= 2:
                pe.wait_ge(sem["row_first"], t - 1)
            ada(t)
        pe.wait_ge(sem["x_in"], 16 * 3)
        for d in range(KD):
            if d >= 2:
                pe.wait_ge(sem["x_row"], 2 * (d - 1))
            for b in range(NB):
                o = ax[:, 2 * (d % 2), 0:P] if b == 0 else ax[:, 2 * (d % 2) + 1, P * (b - 1):P * b]
                last = tr(o, xin[:, b, P * d:P * (d + 1)], ident[:, :])
            last.then_inc(sem["x_tr"], 1)
        cols = [(0, 512), (512, 1024), (1024, NT)]
        pe.wait_ge(sem["consts_in"], 16 * 7)
        for n, (a, b) in enumerate(cols):
            if n == 2:
                pe.wait_ge(sem["x_row"], 16)
            mm(mlp_bank(0, n)[:, 0:b - a], w1[:, :], feat[:, a:b], start=True, stop=True).then_inc(sem["mlp_mm"], 1)
            for t in range(4 + 2 * n, 6 + 2 * n):
                pe.wait_ge(sem["row_first"], t - 1)
                ada(t)
        for t in range(10, 4 * ADA_GROUP):
            pe.wait_ge(sem["row_first"], t - 1)
            ada(t)
        for t in range(4 * ADA_GROUP):
            pe.wait_ge(sem["row_first"], t + 1)
            tr(ax[:, 3, 2 * t:2 * t + 2], rows0[0:2, t, :], ident[0:2, 0:2]).then_inc(sem["col_mm"], 1)
        for n, (a, b) in enumerate(cols):
            pe.wait_ge(sem["mlp_sin"], n + 1)
            mm(mlp_bank(1, n)[:, 0:b - a], w2[:, :], h1T[:, a:b], start=True, stop=True).then_inc(sem["mlp_mm"], 1)
        lane = Counts(None)
        due, raised, now, slot_of = lane.due, lane.raised, lane.now, lane.slot_of

        def tile(g, c, blocks, off, moving, event, ready=None):
            t = TILES.index((g, c))
            if t >= 2:
                ev, n = last_read[t - 2]
                pe.wait_ge(sem[ev], due(ev, n))
            s = slot_of(g)
            for kk in range(blocks):
                if ready:
                    ready(kk)
                for n, (w, lo) in enumerate(((whi[s], False), (whi[s], True), (wlo[s], False))):
                    for hf in range(2):
                        last = mm(gp[:, 2 * (t % 2) + hf, 0:HALF],
                                  w[:, off + P * kk:off + P * (kk + 1)],
                                  moving(kk, lo)[:, hf * HALF:(hf + 1) * HALF],
                                  start=kk == 0 and n == 0, stop=kk == blocks - 1 and n == 2)
            last.then_inc(sem[event], raised(event))

        def both(g, moving, event, ready):
            t0, s = TILES.index((g, 0)), slot_of(g)
            for ev, n in last_read[max(t0 - 2, 0):t0]:
                pe.wait_ge(sem[ev], due(ev, n))
            for kk in range(KD):
                ready(kk)
                for c in range(2):
                    for n, (w, lo) in enumerate(((whi[s], False), (whi[s], True), (wlo[s], False))):
                        for hf in range(2):
                            last = mm(gp[:, 2 * ((t0 + c) % 2) + hf, 0:HALF],
                                      w[:, P * (KD * c + kk):P * (KD * c + kk + 1)],
                                      moving(kk, lo)[:, hf * HALF:(hf + 1) * HALF],
                                      start=kk == 0 and n == 0, stop=kk == KD - 1 and n == 2)
                    if kk == KD - 1:
                        last.then_inc(sem[event], raised(event))

        h_mov = lambda kk, lo: (hlo if lo else hhi)[:, kk, :]

        def h_gemm(g, tiles, event, base=None):
            pe.wait_ge(sem["w_split"], due("w_split", g + 1))
            if base is None:
                for c in range(tiles):
                    tile(g, c, KD, c * KD * P, h_mov, event)
            else:
                both(g, h_mov, event, lambda kk: pe.wait_ge(sem["h_ready"], due("h_ready", base + kk + 1)))

        def qk(b, n0, n1):
            for n in range(n0, n1):
                j, gr = n // 2, n % 2
                seq = NH * b + n
                if seq >= 4:
                    pe.wait_ge(sem["qk_out"], due("qk_out", seq - 3))
                if b and n == 3:
                    pe.wait_ge(sem["at_lo"], due("at_lo", b))
                pr = slice(HD * gr, HD * (gr + 1))
                at = 0
                for kd, f, m in KEYS[b]:
                    rhs = {"own": lambda: k[pr, 0, CTX], "ctx": lambda: kcT[pr, :],
                           "lat": lambda: k[pr, 0, L0 + P * f:L0 + P * (f + m)]}[kd]()
                    last = mm(ax[:, n % 4, at:at + P * m], q[pr, j, tok(b)], rhs, start=True, stop=True)
                    at += P * m
                last.then_inc(sem["qk_mm"], raised("qk_mm"))

        row_out = lambda t: "row_dve" if t % 2 else "row_act"

        def ada_col(t):
            pe.wait_ge(sem[row_out(t)], (t - 2 * ADA_FIRST) // 2 + 1)
            at = ADA_AT + 2 * (t % NH)
            tr(gp[:, 2, at:at + 2], rows[0:2, t % 2, :], ident[0:2, 0:2]).then_inc(sem["col_mm"], 1)

        def tpv(b):
            nk = len(key_blocks[b])

            def pv(n):
                seq = NH * b + n
                pe.wait_ge(sem["pt_dve" if n % 2 else "pt_act"], due("pt_dve" if n % 2 else "pt_act", (NH // 2) * b + n // 2 + 1))
                if n == 0 and b:
                    pe.wait_ge(sem["osb_out"], due("osb_out", b))
                for kb, (kd, i) in enumerate(key_blocks[b]):
                    v = cache_v if kd == "ctx" else vtok[:, 0 if kd == "own" else 1 + i, :]
                    last = mm(ax[:, 2, HD * n:HD * (n + 1)], pt[:, n % 2, P * kb:P * (kb + 1)],
                              v[:, HD * (n % 2):HD * (n % 2 + 1)], start=kb == 0, stop=kb == nk - 1)
                last.then_inc(sem["pv_mm"], raised("pv_mm"))

            if L == 0 and b < 4:
                pe.wait_ge(sem["z_acc"], due("z_acc", 2 * b + 3))
            for n in range(NH):
                pe.wait_ge(sem["exp_out"], due("exp_out", NH * b + n + 1))
                if n >= 2:
                    pe.wait_ge(sem["pt_dve" if n % 2 else "pt_act"], due("pt_dve" if n % 2 else "pt_act", (NH // 2) * b + n // 2))
                for kb in range(nk):
                    last = tr(ax[:, n % 2, P * kb:P * (kb + 1)], sc[:, n, P * kb:P * (kb + 1)], ident[:, :])
                last.then_inc(sem["pt_mm"], raised("pt_mm"))
                if L == 0 and b < 4:
                    t = 2 * ADA_FIRST + NH * b + n
                    if n >= 2:
                        pe.wait_ge(sem[row_out(t)], (t - 2 * ADA_FIRST) // 2)
                    ada(t)
                    if n == 1:
                        pe.wait_ge(sem["z_acc"], due("z_acc", 2 * b + 4))
                    if n:
                        ada_col(t - 1)
                if n:
                    pv(n - 1)
            pv(NH - 1)
            if L == 0 and b < 4:
                ada_col(2 * ADA_FIRST + NH * b + NH - 1)

        def to_features(b):
            pe.wait_ge(sem["osb_out"], due("osb_out", b + 1))
            for j in range(4):
                last = tr(ax[:, 3, P * j:P * (j + 1)], osb[:, P * j:P * (j + 1)], ident[:, :])
            last.then_inc(sem["ot_mm"], raised("ot_mm"))

        def u_transposed(b):
            for j in range(NHY):
                last = tr(gp[:, b % 4, P * j:P * (j + 1)], xu[:, j, tok(b)], ident[:, :])
            last.then_inc(sem["ut_mm"], raised("ut_mm"))

        def spectrum(pair_, places, bank, event):
            s = slot_of(gF + 1) if pair_ < 3 else slot_of(gF if event == "gsp_mm" else gF + 3)
            nk = len(places)
            for o in range(2):
                r = 2 * (GSP_PAIRS.index(pair_) if event == "gsp_mm" else pair_) + o
                if r >= 4:
                    pe.wait_ge(sem[event.replace("mm", "out")], due(event.replace("mm", "out"), r - 3))
                for kb, pl in enumerate(places):
                    blk = (4 * pair_ + 2 * o + kb) if pair_ < 3 else (8 * (pair_ - 3) + 4 * o + kb)
                    cols_ = slice(P * blk, P * (blk + 1))
                    for n, (w, v) in enumerate(((whi, vhi), (whi, vlo), (wlo, vhi))):
                        last = mm(bank[:, r % 4, :], w[s][:, cols_], v[:, pl, :],
                                  start=kb == 0 and n == 0, stop=kb == nk - 1 and n == 2)
                last.then_inc(sem[event], raised(event))

        def inverse(pair_, slot, first, final):
            ys = Y_SLOT[pair_]
            pe.wait_ge(sem["y_ready"], due("y_ready", 2 * pair_ + 2))
            for j in range(NHY):
                for o in range(2):
                    at = 512 * (2 * ((pair_ - 1) % 2) + o)
                    for n, (y, w) in enumerate(((yhi, whi), (yhi, wlo), (ylo, whi))):
                        last = mm(ax[:, j, :], y[:, ys, o, P * j:P * (j + 1)], w[slot][:, at:at + 512],
                                  start=first and o == 0 and n == 0, stop=final and o == 1 and n == 2)
            last.then_inc(sem["linv_mm"], raised("linv_mm"))

        def layer_norm(w):
            pe.wait_ge(sem["sum1_out"], due("sum1_out", KD * (w + 1)))
            pe.wait_ge(sem["sum2_out"], due("sum2_out", KD * (w + 1)))
            for i in range(2):
                for b in range(NB):
                    last = mm(ax[:, 3, NB * i + b:NB * i + b + 1], sums[:, i, tok(b)], ones[:, 0:1],
                              start=True, stop=True)
            last.then_inc(sem["stat_mm"], raised("stat_mm"))
            for i in range(2):
                for b in range(NB):
                    pe.wait_ge(sem["diag_out"], due("diag_out", 2 * NB * w + NB * i + b + 1))
                    o = ax[:, 2 + i, P * i:P * (i + 1)] if b == 0 else ax[:, i, P * (b - 1):P * b]
                    last = mm(o, ones[:, :], diag[:, NB * i + b, :], start=True, stop=True)
                last.then_inc(sem["bc_mm"], raised("bc_mm"))

        for L in range(DEPTH):
            lane.start(L)
            h_gemm(0, 2, "qkv_mm", base=0)
            h_gemm(1, 2, "qkv_mm")
            h_gemm(2, 1, "qkv_mm")
            h_gemm(3, 1, "qkv_mm")
            pe.wait_ge(sem["mlp_arg"], 6)
            for r in range(5):
                pe.wait_ge(sem["qkv_out"], due("qkv_out", r + 1))
                if r == 4:
                    h_gemm(4, 2, "z_mm")
                    pe.wait_ge(sem["rot_out"], due("rot_out", 1))
                src = q[:, r, LAT] if r < 4 else k[:, 0, LAT]
                mm(ax[:, r % 4, :], rot[:, :], src, start=True, stop=True).then_inc(sem["rot_mm"], raised("rot_mm"))
            pe.wait_ge(sem["qkv_out"], due("qkv_out", 6))
            pe.wait_ge(sem["rot_out"], due("rot_out", 3))
            for b in range(1, NB):
                last = tr(ax[:, 1, P * (b - 1):P * b], vrow[:, tok(b)], ident[:, :])
            last.then_inc(sem["vt_mm"], raised("vt_mm"))
            tr(ax[:, 2, 0:P], vrow[:, CTX], ident[:, :])
            tr(ax[:, 2, P:2 * P], cache_k, ident[:, :])
            tr(ax[:, 2, 2 * P:3 * P], k[:, 0, CTX], ident[:, :]).then_inc(sem["vt_mm"], raised("vt_mm"))
            pe.wait_ge(sem["rot_out"], due("rot_out", 5))
            pe.wait_ge(sem["vt_out"], due("vt_out", 4))
            qk(0, 0, NH)
            for b in range(NB):
                if L == 0 and b:
                    pe.wait_ge(sem["mod_done"], due("mod_done", 2 + b))
                h_gemm(5 + b, 2, "z_mm")
                tpv(b)
                if b + 1 < NB:
                    pe.wait_ge(sem["pt_act"], due("pt_act", (NH // 2) * (b + 1)))
                    pe.wait_ge(sem["pt_dve"], due("pt_dve", (NH // 2) * (b + 1)))
                    qk(b + 1, 0, 2)
                to_features(b)
                if b + 1 < NB:
                    qk(b + 1, 2, NH)
            pe.wait_ge(sem["z_acc"], due("z_acc", 12))
            pe.wait_ge(sem["xu_ready"], due("xu_ready", 4))
            pe.wait_ge(sem["mod_done"], due("mod_done", 6))
            for b in range(4):
                u_transposed(b)
            pe.wait_ge(sem["mlp_sin"], 6)
            pe.wait_ge(sem["at_lo"], due("at_lo", NB))
            pe.wait_ge(sem["w3_in"], due("w3_in", 16))
            for n in range(10):
                if n >= 4:
                    pe.wait_ge(sem["filt_out"], due("filt_out", n - 3))
                at = P * n if n < 2 else (2 * P if n % 2 == 0 else 2 * P + DEC_SEQ) + P * (n // 2 - 1)
                mm(ax[:, n % 4, :], h2T[:, at:at + P], w3[:, HY_W * (n % 2):HY_W * (n % 2 + 1)],
                           start=True, stop=True).then_inc(sem["filt_mm"], raised("filt_mm"))
            pe.wait_ge(sem["filt_out"], due("filt_out", 10))
            pe.wait_ge(sem["w_split"], due("w_split", gF + 1))
            pe.wait_ge(sem["gs_ready"], due("gs_ready", 6))
            for p_ in GSP_PAIRS:
                if p_ == 4:
                    pe.wait_ge(sem["ut_out"], due("ut_out", 1))
                    u_transposed(4)
                if p_ == 0:
                    pe.wait_ge(sem["w_split"], due("w_split", gF + 2))
                if p_ == 1:
                    pe.wait_ge(sem["gs_ready"], due("gs_ready", 10))
                spectrum(p_, G_V[p_], ax, "gsp_mm")
            pe.wait_ge(sem["ut_out"], due("ut_out", 5))
            for p_ in range(3):
                pe.wait_ge(sem["us_ready"], due("us_ready", 5 + 2 * p_))
                spectrum(p_, U_V[p_], gp, "usp_mm")
            pe.wait_ge(sem["y_ready"], due("y_ready", 2))
            pe.wait_ge(sem["gsp_out"], due("gsp_out", 10))
            s = slot_of(gF + 1)
            for j in range(NHY):
                for o in range(2):
                    cols_ = slice(P * (12 + o), P * (13 + o))
                    for n, (y, w) in enumerate(((yhi, whi), (yhi, wlo), (ylo, whi))):
                        last = mm(ax[:, 0, P * j:P * (j + 1)], y[:, 0, o, P * j:P * (j + 1)], w[s][:, cols_],
                                  start=o == 0 and n == 0, stop=o == 1 and n == 2)
            last.then_inc(sem["cinv_mm"], raised("cinv_mm"))
            pe.wait_ge(sem["cinv_out"], due("cinv_out", 1))
            pe.wait_ge(sem["w_split"], due("w_split", gF + 3))
            inverse(1, slot_of(gF + 2), True, False)
            pe.wait_ge(sem["w_split"], due("w_split", gF + 4))
            spectrum(3, U_V[3], gp, "usp_mm")
            inverse(2, slot_of(gF + 2), False, False)
            spectrum(4, U_V[4], gp, "usp_mm")
            pe.wait_ge(sem["w_split"], due("w_split", gF + 5))
            inverse(3, slot_of(gF + 4), False, False)
            inverse(4, slot_of(gF + 4), False, True)
            for m in range(KD):
                g = at_g("gate", m)
                h_gemm(g, 2, "gate_mm", base=KD if m == 0 else None)
                if m == 0:
                    pe.wait_ge(sem["pads_at"], due("pads_at", 1))
                pe.wait_ge(sem["w_split"], due("w_split", g + 2))
                tile(g + 1, 0, 4, 0, lambda kk, lo: (atl if lo else ath)[:, kk, :], "proj_mm")
                if m == 0:
                    pe.wait_ge(sem["hy_ready"], due("hy_ready", 4))
                tile(g + 1, 1, 4, 4 * P, lambda kk, lo: (hyl if lo else hyh)[:, kk, :], "proj_mm")
            for i in range(4):
                g = at_g("out", i)
                pe.wait_ge(sem["w_split"], due("w_split", g + 1))
                if i == 0:
                    both(g, lambda kk, lo: mlo(kk) if lo else mhi[:, kk, :], "out_mm",
                         lambda kk: pe.wait_ge(sem["m_ready"], due("m_ready", kk + 1)))
                for c in range(2 if i else 0):
                    tile(g, c, KD, c * KD * P, lambda kk, lo: mlo(kk) if lo else mhi[:, kk, :], "out_mm")
            layer_norm(0)
            for hf in range(2):
                for j in range(FH):
                    jj = FH * hf + j
                    h_gemm(at_g("up", jj), 2, "up_mm", base=2 * KD if jj == 0 else None)
                for m in range(KD):
                    g = at_g("down", KD * hf + m)
                    pe.wait_ge(sem["w_split"], due("w_split", g + 1))
                    tile(g, 0, FH, 0, lambda kk, lo: (actl if lo else acth)[:, kk, :], "down_mm",
                         (lambda kk: pe.wait_ge(sem["act_ready"], due("act_ready", FH * hf + kk + 1))) if m == 0 else None)
            layer_norm(1)
        lane.end()
        for b in range(NB):
            pe.wait_ge(sem["ln_x"], due("ln_x", 16))
            pe.wait_ge(sem["ln_norm"], due("ln_norm", 16))
            if b == 4:
                pe.wait_ge(sem["y_out"], 1)
                pe.wait_ge(sem["y_out_act"], 1)
            for d in range(KD):
                last = tr(y_banks(b)[:, d // 4, P * (d % 4):P * (d % 4 + 1)], x[:, d, tok(b)], ident[:, :])
            last.then_inc(sem["y_mm"], 1)

    @block.scalar
    def _(act):
        lane = Counts("act_order")
        due, raised, now, slot_of = lane.due, lane.raised, lane.now, lane.slot_of
        run = nc.scalar.activation
        act.sem_inc(sem["ln_x"], CREDIT["ln_x"])
        act.wait_ge(sem["cond_in"], 16)
        run(cs[:, :, :], cs[:, :, :], ACT.Silu).then_inc(sem["cond_ready"], 1)

        def first_rows(a, b):
            for t in range(a, b):
                act.wait_ge(sem["ada_mm"], t + 1)
                run(rows0[0:2, t, :], gp[0:2, t % 2, ADA_AT:ADA_AT + P], ACT.Copy).then_inc(sem["row_first"], 1)

        def sine(i):
            dst = (h1T, h2T)[i // 3]
            a, b = ((0, 512), (512, 1024), (1024, NT))[i % 3]
            act.wait_ge(sem["mlp_arg"], i + 1)
            run(dst[:, a:b], dst[:, a:b], ACT.Sin).then_inc(sem["mlp_sin"], 1)

        first_rows(0, 6)
        for i in range(3):
            first_rows(6 + 2 * i, 8 + 2 * i)
            sine(i)
        first_rows(12, 16)

        def split(g):
            s = slot_of(g)
            n = width(g)
            st_ = STEP[(lane.layer, "g", g)]
            act.wait_ge(sem[f"raw{st_ % 2}"], 16 * (st_ // 2 + 1))
            if g >= 2:
                ev, m = chunk_done[g - 2]
                act.wait_ge(sem[ev], due(ev, m))
            else:
                act.wait_ge(sem["down_mm"], due("down_mm", g - 1))
            run(whi[s][:, 0:n], raw[st_ % 2][:, 0:n], ACT.Copy).then_inc(sem["w_hi"], raised("w_hi"))

        def hi(dst, src, ready, n, event):
            act.wait_ge(sem[ready], due(ready, n))
            run(dst, src, ACT.Copy).then_inc(sem[event], raised(event))

        def soft(b):
            nk = len(key_blocks[b]) * P
            act.wait_ge(sem["soft_m"], due("soft_m", b + 1))
            run(small[:, 32:40], small[:, 24:32], ACT.Exp).then_inc(sem["act_order"], raised("act_order"))
            for n in range(NH):
                run(sc[:, n, 0:nk], sc[:, n, 0:nk], ACT.Exp, bias=small[:, 16 + n:17 + n],
                       scale=HD ** -0.5, accum_out=small[:, 40 + n:41 + n]).then_inc(sem["exp_out"], raised("exp_out"))

        def tpv(b):
            nk = len(key_blocks[b]) * P
            for n in range(0, NH, 2):
                act.wait_ge(sem["pt_mm"], due("pt_mm", NH * b + n + 1))
                if NH * b + n >= 2:
                    act.wait_ge(sem["pv_mm"], due("pv_mm", NH * b + n - 1))
                run(pt[:, 0, 0:nk], ax[:, 0, 0:nk], ACT.Copy).then_inc(sem["pt_act"], raised("pt_act"))
                if L == 0 and b < 4:
                    t = 2 * ADA_FIRST + NH * b + n
                    act.wait_ge(sem["ada_mm"], t + 1)
                    if t >= 2 * ADA_FIRST + 2:
                        act.wait_ge(sem["col_mm"], t - 1)
                    run(rows[0:2, 0, :], gp[0:2, 0, ADA_AT:ADA_AT + P], ACT.Copy).then_inc(sem["row_act"], 1)
            act.wait_ge(sem["ot_mm"], due("ot_mm", b + 1))
            run(ath[:, :, tok(b)], ax[:, 3, :].rearrange("p (j t) -> p j t", j=4), ACT.Copy).then_inc(sem["at_hi"], raised("at_hi"))

        def squares(m, event, n):
            act.wait_ge(sem[event], due(event, n))
            k_ = n_sq[0]
            n_sq[0] += 1
            if k_ >= 2:
                act.wait_ge(sem["sum2_out"], due("sum2_out", k_ - 1))
            run(sq[:, m % 2, :], x[:, m, :], ACT.Square).then_inc(sem["sq_out"], raised("sq_out"))

        for L in range(DEPTH):
            lane.start(L)
            n_sq = [0]
            act.wait_ge(sem["params_in"], due("params_in", 16))
            if L == 0:
                split(0)
                act.wait_ge(sem["mlp_mm"], 6)
                for d in range(KD):
                    hi(hhi[:, d, :], hsrc[:, d % 2, :], "h_src", d + 1, "h_hi")
            for g in range(4):
                split(g + 1)
                for t in ((0, 1), (2, 3), (4,), (5,))[g]:
                    act.wait_ge(sem["qkv_mm"], due("qkv_mm", t + 1))
                    dst = q[:, t, :] if t < 4 else k[:, 0, :] if t == 4 else vrow
                    run(two(dst), pair(t), ACT.Copy).then_inc(sem["qkv_out"], raised("qkv_out"))
                if L == 0 and g:
                    sine(2 + g)
            for i in range(6):
                split(5 + i)
                for c in range(2):
                    t = 2 * i + c
                    act.wait_ge(sem["z_mm"], due("z_mm", t + 1))
                    if i:
                        act.wait_ge(sem["z_out"], due("z_out", 2 * i))
                        if i < 5:
                            act.wait_ge(sem["xu_ready"], due("xu_ready", i))
                    src = pair(t)
                    run(two(zt[:, c, :]), src, ACT.Copy).then_inc(sem["z_raw"], raised("z_raw"))
                    dst = ca[:, c, :] if i < 4 else x0c[:, 2 * (i - 4) + c, :]
                    zi = (4 + i, 8 + i)[c] if i < 4 else 2 * (i - 4) + c
                    run(two(dst), src, ACT.Identity, bias=parc("hy_b", zi),
                           scale=parc("hy_w", 3 * zi + 1)).then_inc(sem["z_acc"], raised("z_acc"))
                if i == 0:
                    act.wait_ge(sem["vt_mm"], due("vt_mm", 1))
                    run(vtok[:, 1:NB, :], ax[:, 1, :].rearrange("p (b t) -> p b t", t=P), ACT.Copy).then_inc(sem["vt_out"], raised("vt_out"))
                    act.wait_ge(sem["vt_mm"], due("vt_mm", 2))
                    run(vtok[:, 0, :], ax[:, 2, 0:P], ACT.Copy).then_inc(sem["vt_out"], raised("vt_out"))
                    run(kcT[:, :], ax[:, 2, P:2 * P], ACT.Copy).then_inc(sem["vt_out"], raised("vt_out"))
                    run(kout[:, :], ax[:, 2, 2 * P:3 * P], ACT.Copy).then_inc(sem["vt_out"], raised("vt_out"))
                if i:
                    tpv(i - 1)
                if i < NB:
                    soft(i)
            split(gF + 1)
            act.wait_ge(sem["z_mm"], due("z_mm", 12))
            fsrc = [ssum[0], dreg[:, :]] + [dreg[:, :]] * 4 + [prod[:, 0, :], prod[:, 1, :]] * 2
            for n, v in enumerate(GS_V):
                hi(vhi[:, v, :], fsrc[n], "gs_src", n + 1, "gs_hi")
            for b in range(NB):
                act.wait_ge(sem["ut_mm"], due("ut_mm", b + 1))
                run(ureg[:, b - 1, :] if b else uctx[:, :], gp[:, b % 4, :], ACT.Copy).then_inc(sem["ut_out"], raised("ut_out"))

            def u_hi(a, b):
                for n in range(a, b):
                    src = ureg[:, n, :] if n < 4 else uctx[:, :] if n == 4 else ufold[:, n - 5, :]
                    hi(vhi[:, US_V[n], :], src, *(("ut_out", 5) if n < 5 else ("us_src", n - 4)), "us_hi")

            for r in range(10):
                act.wait_ge(sem["gsp_mm"], due("gsp_mm", r + 1))
                run(gsp[:, GSP_PAIRS[r // 2], r % 2, :], ax[:, r % 4, :], ACT.Copy).then_inc(sem["gsp_out"], raised("gsp_out"))
                if r == 3:
                    u_hi(0, 4)
                    split(gF + 2)
                if r >= 5 and r % 2:
                    u_hi(*((4, 5), (5, 7), (7, 9))[(r - 5) // 2])
            for p_ in range(PAIRS):
                for o in range(2):
                    r = 2 * p_ + o
                    act.wait_ge(sem["usp_mm"], due("usp_mm", r + 1))
                    if p_:
                        act.wait_ge(sem["y_ready"], due("y_ready", 2 * p_))
                    run(us[:, o, :], gp[:, r % 4, :], ACT.Copy).then_inc(sem["usp_out"], raised("usp_out"))
                for o in range(2):
                    if p_ == 2:
                        act.wait_ge(sem["cinv_mm"], due("cinv_mm", 1))
                    if p_ >= 3:
                        act.wait_ge(sem["linv_mm"], due("linv_mm", p_ - 2))
                    hi(yhi[:, Y_SLOT[p_], 1 - o, :], us[:, o, :], "y_src", 2 * p_ + o + 1, "y_hi")
                if p_ == 1:
                    split(gF + 3)
                if p_ == 3:
                    split(gF + 4)
            split(gF + 5)
            act.wait_ge(sem["usp_mm"], due("usp_mm", 10))
            act.wait_ge(sem["pads_h"], due("pads_h", 2))
            for d in range(KD):
                if d >= 2:
                    act.wait_ge(sem["h_ready"], due("h_ready", KD + d - 1))
                for gr, cols_ in enumerate((CTX, LAT)):
                    run(hsrc[:, d % 2, cols_], x[:, d, cols_], ACT.Identity, bias=mod[:, SH1 + d, gr:gr + 1],
                        scale=mod[:, SC1 + d, gr:gr + 1]).then_inc(sem["act_order"], raised("act_order"))
                act.wait_ge(sem["act_order"], now("act_order"))
                run(hhi[:, d, :], hsrc[:, d % 2, :], ACT.Copy).then_inc(sem["h_hi"], raised("h_hi"))
            split(gF + 6)
            for m in range(KD):
                g = at_g("gate", m)
                if m:
                    split(g + 1)
                for c in range(2):
                    act.wait_ge(sem["gate_mm"], due("gate_mm", 2 * m + c + 1))
                    act.wait_ge(sem["m_ready"], due("m_ready", m)) if m else act.wait_ge(sem["h_ready"], due("h_ready", 2 * KD))
                    t = TILES.index((g, c))
                    run(two(gates[:, c, :]), pair(t), ACT.Sigmoid).then_inc(sem["gate_out"], raised("gate_out"))
                if m == 0:
                    for j in range(NHY):
                        hi(hyh[:, j, :], xu[:, j, :], "hy_src", j + 1, "hy_hi")
                split(g + 2)
                hi(mhi[:, m, :], gates[:, 0, :], "m_src", m + 1, "m_hi")
            for i in range(4):
                split(at_g("out", i) + 1)
                for c in range(2):
                    squares(2 * i + c, "out_out", 2 * i + c + 1)
            for w in range(2):
                if w and L + 1 < DEPTH:
                    lane.start(L + 1)
                    split(0)
                    lane.start(L)
                act.wait_ge(sem["ln_var"], due("ln_var", w + 1))
                run(small[:, 71:76], small[:, 66:71], ACT.Sqrt).then_inc(sem["ln_sqrt"], raised("ln_sqrt"))
                act.wait_ge(sem["bc_mm"], due("bc_mm", 2 * w + 2))
                run(gz[:, 0, CTX], ax[:, 3, P:2 * P], ACT.Copy).then_inc(sem["ln_shift"], raised("ln_shift"))
                run(gz[:, 0, LAT], ax[:, 1, :], ACT.Copy).then_inc(sem["ln_shift"], raised("ln_shift"))
                following = w == 0 or L + 1 < DEPTH
                for d in range(KD + following):
                    if d < KD:
                        act.wait_ge(sem["ln_norm"], due("ln_norm", KD * w + d + 1))
                        ln = f"ln{w + 1}_"
                        run(x[:, d, :], x[:, d, :], ACT.Identity, bias=parc(ln + "b", d),
                               scale=parc(ln + "g", d)).then_inc(sem["ln_x"], raised("ln_x"))
                    if following and d:
                        hi(hhi[:, d - 1, :], hsrc[:, (d - 1) % 2, :], "h_src", (1 + w) * KD + d, "h_hi")
                if w:
                    break
                for hf in range(2):
                    for j in range(FH):
                        jj = FH * hf + j
                        g = at_g("up", jj)
                        split(g + 1)
                        if L + 1 < DEPTH and jj == 0:
                            act.wait_ge(sem["cond_rows_in"], 16 * (L + 1))
                            run(crow[:, :, :], crow[:, :, :], ACT.Silu).then_inc(sem["cond_rows"], 1)
                        sl = jj % 2
                        src = pair(TILES.index((g, 0)))
                        act.wait_ge(sem["up_mm"], due("up_mm", 2 * jj + 1))
                        if jj >= 2:
                            act.wait_ge(sem["act_ready"], due("act_ready", jj - 1))
                        run(two(gz[:, sl, :]), src, ACT.Copy).then_inc(sem["up_raw"], raised("up_raw"))
                        run(two(ga[:, sl, :]), src, ACT.Identity, bias=parc("ff_b", jj),
                               scale=parc("ff_w", 3 * jj + 1)).then_inc(sem["up_acc"], raised("up_acc"))
                        act.wait_ge(sem["up_taps"], due("up_taps", jj + 1))
                        run(ga[:, sl, :], ga[:, sl, :], ACT.Gelu).then_inc(sem["up_gelu"], raised("up_gelu"))
                        if hf and j == 0:
                            act.wait_ge(sem["down_mm"], due("down_mm", KD))
                        hi(acth[:, j, :], ga[:, sl, :], "up_out", jj + 1, "act_hi")
                    for m in range(KD):
                        g = at_g("down", KD * hf + m)
                        if g + 1 < NG:
                            split(g + 1)
                        if hf:
                            squares(m, "down_out", KD + m + 1)
        lane.end()
        for b in range(NB):
            act.wait_ge(sem["y_mm"], b + 1)
            run(yout[:, b, 512:1024], y_banks(b)[:, 1, :], ACT.Copy).then_inc(sem["y_out_act"], 1)

    @block.vector
    def _(dve):
        lane = Counts("dve_order")
        due, raised, now, slot_of = lane.due, lane.raised, lane.now, lane.slot_of
        V = nc.vector
        TT, TS, STT = V.tensor_tensor, V.tensor_scalar, V.scalar_tensor_tensor
        for n in ("w_split", "m_ready", "h_ready"):
            dve.sem_inc(sem[n], CREDIT[n])
        dve.wait_ge(sem["consts_in"], 16 * 7)
        V.tensor_copy(mask[:, :], mask_in[:, :]).then_inc(sem["mask_done"], 1)
        dve.wait_ge(sem["mask_done"], 1)
        dve.wait_ge(sem["x_zero"], 1)
        for d in range(KD):
            dve.wait_ge(sem["x_tr"], d + 1)
            V.tensor_copy(x[:, d, CTX], ax[:, 2 * (d % 2), 0:P]).then_inc(sem["x_row"], 1)
            V.tensor_copy(x[:, d, LAT], ax[:, 2 * (d % 2) + 1, :]).then_inc(sem["x_row"], 1)
        n_ord = [0]

        def sine_arg(lay, n):
            a, b = ((0, 512), (512, 1024), (1024, NT))[n]
            dve.wait_ge(sem["mlp_mm"], 3 * lay + n + 1)
            arg, turns = (h1T, h2T)[lay][:, a:b], (turns2[:, 0:b - a] if lay else prod[:, 0, 0:b - a])
            ops = [lambda: TS(arg, mlp_bank(lay, n)[:, 0:b - a], mlpv[:, 2 * lay:2 * lay + 1],
                              mlpv[:, 2 * lay + 1:2 * lay + 2], ALU.add, ALU.mult),
                   lambda: TS(turns, arg, 1 / (2 * math.pi), MAGIC, ALU.mult, ALU.add),
                   lambda: TS(turns, turns, -MAGIC, None, ALU.add)]
            ops += [lambda c=c: STT(arg, turns, -c, arg, ALU.mult, ALU.add) for c in TWO_PI_PARTS]
            for op in ops:
                op().then_inc(sem["mlp_order"], 1)
                n_ord[0] += 1
                dve.wait_ge(sem["mlp_order"], n_ord[0])
            TS(arg, arg, 3.1415925, -3.1415925, ALU.min, ALU.max).then_inc(sem["mlp_arg"], 1)

        for n in range(3):
            sine_arg(0, n)
        dve.wait_ge(sem["mlp_arg"], 3)

        b_ada = lambda v: par[:, PAR["b_ada"] + KD * v:PAR["b_ada"] + KD * (v + 1)]

        def modulation(v, sums_, bias):
            STT(mod[:, KD * v:KD * (v + 1), :], sums_.rearrange("p (j g) -> p j g", g=2),
                float(v in (1, 4)), bias.unsqueeze(2).to_broadcast([P, KD, 2]), ALU.add, ALU.add).then_inc(sem["mod_done"], raised("mod_done"))

        def ada_t(c):
            n = STEP[(L + 1, "ada", c)]
            dve.wait_ge(sem[f"raw{n % 2}"], 16 * (n // 2 + 1))
            for t in (2 * c, 2 * c + 1):
                for gr in range(2):
                    k_ = 4 * ADA_STEPS * L + 2 * t + gr
                    if 2 * t + gr >= 2:
                        dve.wait_ge(sem["ada_t"], k_ - 1)
                    to = small[:, 2 * (t - G2) + gr:2 * (t - G2) + gr + 1] if t >= G2 else mod[:, t, gr:gr + 1]
                    V.tensor_tensor_reduce(out=ax[:, 2 * gr:2 * gr + 2, :].rearrange("p a b -> p (a b)"),
                                           in0=raw[n % 2][:, D_MODEL * (t % 2):D_MODEL * (t % 2 + 1)],
                                           in1=crow[:, gr, :], scale=1.0, scalar=0.0, op0=ALU.mult,
                                           op1=ALU.add, accum_out=to).then_inc(sem["ada_t"], 1)

        def split(g):
            s, n = slot_of(g), width(g)
            dve.wait_ge(sem["w_hi"], due("w_hi", g + 1))
            TT(wlo[s][:, 0:n], raw[STEP[(lane.layer, "g", g)] % 2][:, 0:n], f32(whi[s][:, 0:n]), ALU.subtract).then_inc(sem["w_split"], raised("w_split"))

        def lo(dst, src, hi_, event_hi, n, event):
            dve.wait_ge(sem[event_hi], due(event_hi, n))
            TT(dst, src, f32(hi_), ALU.subtract).then_inc(sem[event], raised(event))

        def h_src(n, d, sh, sc_):
            if d == 0:
                dve.wait_ge(sem["pads_h"], due("pads_h", n + 1))
            if d >= 2:
                dve.wait_ge(sem["h_ready"], due("h_ready", KD * n + d - 1))
            for gr, cols_ in enumerate((CTX, LAT)):
                TS(hsrc[:, d % 2, cols_], x[:, d, cols_], mod[:, sc_ + d, gr:gr + 1],
                      mod[:, sh + d, gr:gr + 1], ALU.mult, ALU.add).then_inc(sem["h_src" if gr else "dve_order"], raised("h_src" if gr else "dve_order"))

        def h_lo(n, d):
            lo(hlo[:, d, :], hsrc[:, d % 2, :], hhi[:, d, :], "h_hi", KD * n + d + 1, "h_ready")

        def h_all(n, sh, sc_):
            for d in range(KD + 1):
                if d < KD:
                    h_src(n, d, sh, sc_)
                if d:
                    h_lo(n, d - 1)

        def taps(rows, accs, ws, event):
            for tap, a in ((0, 0), (2, 2)):
                for i, (z, acc, w) in enumerate(zip(rows, accs, ws)):
                    if tap and i == 0:
                        dve.wait_ge(sem["dve_order"], now("dve_order"))
                    STT(acc[:, 1:ROW - 1], z[:, a:a + ROW - 2], w(tap), acc[:, 1:ROW - 1],
                           ALU.mult, ALU.add).then_inc(sem[event if tap else "dve_order"], raised(event if tap else "dve_order"))

        def conv(i):
            dve.wait_ge(sem["z_acc"], due("z_acc", 2 * i + 2))
            if i < 4:
                taps([zt[:, c, :] for c in range(2)], [ca[:, c, :] for c in range(2)],
                     [lambda tp, z=z: parc("hy_w", 3 * z + tp) for z in (4 + i, 8 + i)], "z_out")
                dve.wait_ge(sem["z_out"], now("z_out"))
                TT(xu[:, i, :], ca[:, 0, :], ca[:, 1, :], ALU.mult).then_inc(sem["xu_ready"], raised("xu_ready"))
            else:
                z0 = 2 * (i - 4)
                taps([zt[:, c, :] for c in range(2)], [x0c[:, z0 + c, :] for c in range(2)],
                     [lambda tp, z=z: parc("hy_w", 3 * z + tp) for z in (z0, z0 + 1)], "z_out")

        def rope(r):
            row = q[:, r, LAT] if r < 4 else k[:, 0, LAT]
            tmp = scf[:, 1024 + 512 * (r % 2):1536 + 512 * (r % 2)]
            dve.wait_ge(sem["rot_mm"], due("rot_mm", r + 1))
            dve.wait_ge(sem["qkv_out"], due("qkv_out", min(r + 1, 5)))
            TT(row, row, trig[:, 0, :], ALU.mult).then_inc(sem["dve_order"], raised("dve_order"))
            TT(tmp, ax[:, r % 4, :], trig[:, 1, :], ALU.mult).then_inc(sem["dve_order"], raised("dve_order"))
            dve.wait_ge(sem["dve_order"], now("dve_order"))
            TT(row, row, tmp, ALU.add).then_inc(sem["rot_out"], raised("rot_out"))

        def scores(b, n0, n1):
            nk = len(key_blocks[b]) * P
            for n in range(n0, n1):
                dve.wait_ge(sem["qk_mm"], due("qk_mm", NH * b + n + 1))
                V.tensor_tensor_reduce(out=sc[:, n, 0:nk], in0=ax[:, n % 4, 0:nk],
                                          in1=mask[:, P * MASK_AT[b]:P * MASK_AT[b] + nk], scale=1.0,
                                          scalar=-3e38, op0=ALU.add, op1=ALU.max,
                                          accum_out=small[:, n:n + 1]).then_inc(sem["qk_out"], raised("qk_out"))

        def soft(b):
            if b:
                dve.wait_ge(sem["at_lo"], now("at_lo"))
            else:
                dve.wait_ge(sem["vt_mm"], due("vt_mm", 2))
                dve.wait_ge(sem["rot_out"], now("rot_out"))
                scores(0, 0, 2)
            scores(b, 2, NH)
            dve.wait_ge(sem["qk_out"], now("qk_out"))
            sink = par[:, PAR["sink"]:PAR["sink"] + NH]
            STT(small[:, 8:16], small[:, 0:8], HD ** -0.5, sink, ALU.mult, ALU.max).then_inc(sem["dve_order"], raised("dve_order"))
            dve.wait_ge(sem["dve_order"], now("dve_order"))
            TS(small[:, 16:24], small[:, 8:16], -1.0, None, ALU.mult).then_inc(sem["dve_order"], raised("dve_order"))
            TT(small[:, 24:32], sink, small[:, 8:16], ALU.subtract).then_inc(sem["soft_m"], raised("soft_m"))

        def tpv(b):
            nk = len(key_blocks[b]) * P
            dve.wait_ge(sem["exp_out"], due("exp_out", NH * (b + 1)))
            TT(small[:, 48:56], small[:, 40:48], small[:, 32:40], ALU.add).then_inc(sem["dve_order"], raised("dve_order"))
            dve.wait_ge(sem["dve_order"], now("dve_order"))
            V.reciprocal(small[:, 56:64], small[:, 48:56]).then_inc(sem["dve_order"], raised("dve_order"))
            for n in range(1, NH, 2):
                dve.wait_ge(sem["pt_mm"], due("pt_mm", NH * b + n + 1))
                if NH * b + n >= 2:
                    dve.wait_ge(sem["pv_mm"], due("pv_mm", NH * b + n - 1))
                V.tensor_copy(pt[:, 1, 0:nk], ax[:, 1, 0:nk]).then_inc(sem["pt_dve"], raised("pt_dve"))
                if b == 4:
                    tap, c = 2 * (n // 4), n // 2 % 2
                    if n == 1:
                        dve.wait_ge(sem["z_acc"], due("z_acc", 12))
                    if n == 5:
                        dve.wait_ge(sem["dve_order"], now("dve_order"))
                    acc = x0c[:, 2 + c, 1:ROW - 1]
                    event = "z_out" if tap else "dve_order"
                    STT(acc, zt[:, c, tap:tap + ROW - 2], parc("hy_w", 3 * (2 + c) + tap), acc,
                        ALU.mult, ALU.add).then_inc(sem[event], raised(event))
                if L == 0 and b < 4:
                    t = 2 * ADA_FIRST + NH * b + n
                    dve.wait_ge(sem["ada_mm"], t + 1)
                    if t >= 2 * ADA_FIRST + 2:
                        dve.wait_ge(sem["col_mm"], t - 1)
                    V.tensor_copy(rows[0:2, 1, :], gp[0:2, 1, ADA_AT:ADA_AT + P]).then_inc(sem["row_dve"], 1)
            dve.wait_ge(sem["pv_mm"], due("pv_mm", NH * (b + 1)))
            if b:
                dve.wait_ge(sem["ot_mm"], due("ot_mm", b))
            TT(osb[:, :].rearrange("p (n d) -> p n d", d=HD),
                  ax[:, 2, :].rearrange("p (n d) -> p n d", d=HD),
                  small[:, 56:64].unsqueeze(2).to_broadcast([P, NH, HD]), ALU.mult).then_inc(sem["osb_out"], raised("osb_out"))
            if b + 1 < NB:
                scores(b + 1, 0, 2)
            dve.wait_ge(sem["at_hi"], due("at_hi", b + 1))
            TT(atl[:, :, tok(b)], ax[:, 3, :].rearrange("p (j t) -> p j t", j=4),
                  f32(ath[:, :, tok(b)]), ALU.subtract).then_inc(sem["at_lo"], raised("at_lo"))
            if L == 0 and b < 4:
                dve.wait_ge(sem["col_mm"], 2 * ADA_FIRST + NH * (b + 1))
                modulation(2 + b, gp[:, 2, ADA_AT:ADA_AT + 2 * KD], b_ada(2 + b))

        def residual(m, t, gate, event):
            for n, (gr, bank, a, b) in enumerate(((0, 0, C0, C0 + SEQ), (1, 0, L0, HALF), (1, 1, 0, HALF - 1))):
                xs = x[:, m, HALF * bank + a:HALF * bank + b]
                STT(xs, gp[:, 2 * (t % 2) + bank, a:b], mod[:, gate + m, gr:gr + 1], xs,
                       ALU.mult, ALU.add).then_inc(sem[event if n == 2 else "dve_order"], raised(event if n == 2 else "dve_order"))

        def sum2(m, n):
            dve.wait_ge(sem["sq_out"], due("sq_out", n))
            if m == 0:
                V.tensor_copy(sums[:, 1, :], sq[:, 0, :]).then_inc(sem["sum2_out"], raised("sum2_out"))
            else:
                dve.wait_ge(sem["sum2_out"], now("sum2_out"))
                TT(sums[:, 1, :], sums[:, 1, :], sq[:, m % 2, :], ALU.add).then_inc(sem["sum2_out"], raised("sum2_out"))

        for L in range(DEPTH):
            lane.start(L)
            dve.wait_ge(sem["params_in"], due("params_in", 16))
            if L == 0:
                dve.wait_ge(sem["col_mm"], 4 * ADA_GROUP)
                for v in range(2):
                    modulation(v, ax[:, 3, 2 * KD * v:2 * KD * (v + 1)], b_ada(v))
                dve.wait_ge(sem["mod_done"], now("mod_done"))
                split(0)
                h_all(0, SH1, SC1)
            else:
                for v in range(2, 6):
                    modulation(v, mod[:, KD * v:KD * (v + 1), :].rearrange("p j g -> p (j g)") if v < 5 else
                               small[:, 0:2 * KD], b_ada(v))
                dve.wait_ge(sem["mod_done"], now("mod_done"))
            for g in range(4):
                split(g + 1)
                if L == 0 and g < 3:
                    sine_arg(1, g)
            dve.wait_ge(sem["trig_in"], due("trig_in", 16))
            for r in range(4):
                rope(r)
            for i in range(6):
                if i:
                    conv(i - 1)
                split(5 + i)
                if i == 0:
                    rope(4)
                if i:
                    tpv(i - 1)
                if i < NB:
                    soft(i)
            split(gF + 1)
            dve.wait_ge(sem["pads_at"], due("pads_at", 1))
            for n in range(10):
                dve.wait_ge(sem["filt_mm"], due("filt_mm", n + 1))
                dve.wait_ge(sem["win_in"], due("win_in", 16 * (1 if n < 4 else n // 2)))
                TT(prod[:, n % 2, :], ax[:, n % 4, :], filt[:, 2 + n % 4, :], ALU.mult).then_inc(sem["filt_out"], raised("filt_out"))
                if n % 2 == 0:
                    continue
                dve.wait_ge(sem["filt_out"], now("filt_out"))
                b = max(n // 2 - 1, 0)
                event = "gs_src" if n == 1 else "dve_order"
                TT(ssum[b], prod[:, 0, :], prod[:, 1, :], ALU.add).then_inc(sem[event], raised(event))
                TT(dreg[:, :], prod[:, 0, :], prod[:, 1, :], ALU.subtract).then_inc(sem["gs_src"], raised("gs_src"))
                if n == 1:
                    lo(vlo[:, 0, :], ssum[0], vhi[:, 0, :], "gs_hi", 1, "gs_ready")
                nn = n // 2 + 2
                v = GS_V[nn - 1]
                lo(vlo[:, v, :], dreg[:, :], vhi[:, v, :], "gs_hi", nn, "gs_ready")
                dve.wait_ge(sem["gs_ready"], now("gs_ready"))
            for n in range(4):
                a, b, op = ((0, 2, ALU.add), (1, 3, ALU.add), (0, 2, ALU.subtract), (1, 3, ALU.subtract))[n]
                TT(prod[:, n % 2, :], ssum[a], ssum[b], op).then_inc(sem["gs_src"], raised("gs_src"))
                lo(vlo[:, 2 + n, :], prod[:, n % 2, :], vhi[:, 2 + n, :], "gs_hi", 7 + n, "gs_ready")
                dve.wait_ge(sem["gs_ready"], now("gs_ready"))
            dve.wait_ge(sem["ut_out"], due("ut_out", 5))
            for n in range(4):
                a, b, op = ((0, 2, ALU.add), (1, 3, ALU.add), (0, 2, ALU.subtract), (1, 3, ALU.subtract))[n]
                TT(ufold[:, n, :], ureg[:, a, :], ureg[:, b, :], op).then_inc(sem["us_src"], raised("us_src"))
            for n in range(9):
                if n == 4:
                    split(gF + 2)
                src = ureg[:, n, :] if n < 4 else uctx[:, :] if n == 4 else ufold[:, n - 5, :]
                if n == 5:
                    dve.wait_ge(sem["us_src"], now("us_src"))
                lo(vlo[:, US_V[n], :], src, vhi[:, US_V[n], :], "us_hi", n + 1, "us_ready")
            for p_ in range(PAIRS):
                dve.wait_ge(sem["usp_out"], due("usp_out", 2 * p_ + 2))
                gr, gi = gsp[:, p_, 0, :], gsp[:, p_, 1, :]
                dve.wait_ge(sem["gsp_out"], due("gsp_out", 10))
                TT(prod[:, 0, :], us[:, 0, :], gr, ALU.mult).then_inc(sem["dve_order"], raised("dve_order"))
                TT(prod[:, 1, :], us[:, 1, :], gi, ALU.mult).then_inc(sem["dve_order"], raised("dve_order"))
                dve.wait_ge(sem["dve_order"], now("dve_order"))
                TT(us[:, 0, :], us[:, 0, :], gi, ALU.mult).then_inc(sem["dve_order"], raised("dve_order"))
                TT(us[:, 1, :], us[:, 1, :], gr, ALU.mult).then_inc(sem["dve_order"], raised("dve_order"))
                dve.wait_ge(sem["dve_order"], now("dve_order"))
                real = p_ < 2
                TT(us[:, 0, :], us[:, 0, :], us[:, 1, :], ALU.add).then_inc(sem["dve_order" if real else "y_src"], raised("dve_order" if real else "y_src"))
                if real:
                    dve.wait_ge(sem["dve_order"], now("dve_order"))
                    V.tensor_copy(us[0:1, 0, :], prod[0:1, 1, :]).then_inc(sem["y_src"], raised("y_src"))
                dve.wait_ge(sem["y_src"], now("y_src"))
                TT(us[:, 1, :], prod[:, 0, :], prod[:, 1, :], ALU.subtract).then_inc(sem["dve_order" if real else "y_src"], raised("dve_order" if real else "y_src"))
                if real:
                    dve.wait_ge(sem["dve_order"], now("dve_order"))
                    V.tensor_copy(us[0:1, 1, :], prod[0:1, 0, :]).then_inc(sem["y_src"], raised("y_src"))
                for o in range(2):
                    ys = Y_SLOT[p_]
                    lo(ylo[:, ys, 1 - o, :], us[:, o, :], yhi[:, ys, 1 - o, :], "y_hi", 2 * p_ + o + 1, "y_ready")
                if p_ == 1:
                    dve.wait_ge(sem["cinv_mm"], due("cinv_mm", 1))
                    for j in range(NHY):
                        STT(xu[:, j, CTX], xu[:, j, CTX], parc("hy_bias", j), ax[:, 0, P * j:P * (j + 1)],
                               ALU.mult, ALU.add).then_inc(sem["cinv_out" if j == 3 else "dve_order"], raised("cinv_out" if j == 3 else "dve_order"))
                    dve.wait_ge(sem["cinv_out"], now("cinv_out"))
                    TT(xu[:, :, CTX], xu[:, :, CTX], x0c[:, :, CTX], ALU.mult).then_inc(sem["dve_order"], raised("dve_order"))
                    split(gF + 3)
                if p_ == 3:
                    split(gF + 4)
            split(gF + 5)
            for d in range(KD):
                h_lo(1, d)
                if 2 <= d < 2 + NHY:
                    j = d - 2
                    dve.wait_ge(sem["linv_mm"], due("linv_mm", 4))
                    STT(xu[:, j, LAT], xu[:, j, LAT], parc("hy_bias", j), ax[:, j, :], ALU.mult, ALU.add)\
                        .then_inc(sem["dve_order"], raised("dve_order"))
                if d >= KD - NHY:
                    j = d - KD + NHY
                    dve.wait_ge(sem["dve_order"], now("dve_order"))
                    TT(xu[:, j, LAT], xu[:, j, LAT], x0c[:, j, LAT], ALU.mult).then_inc(sem["hy_src"], raised("hy_src"))
            split(gF + 6)
            for j in range(NHY):
                lo(hyl[:, j, :], xu[:, j, :], hyh[:, j, :], "hy_hi", j + 1, "hy_ready")
            for m in range(KD):
                g = at_g("gate", m)
                if m:
                    split(g + 1)
                split(g + 2)
                for c in range(2):
                    dve.wait_ge(sem["gate_out"], due("gate_out", 2 * m + c + 1))
                    dve.wait_ge(sem["proj_mm"], due("proj_mm", 2 * m + c + 1))
                    TT(two(gates[:, c, :]), two(gates[:, c, :]), pair(TILES.index((g + 1, c))), ALU.mult).then_inc(sem["proj_out"], raised("proj_out"))
                dve.wait_ge(sem["proj_out"], now("proj_out"))
                TT(gates[:, 0, :], gates[:, 0, :], gates[:, 1, :], ALU.add).then_inc(sem["m_src"], raised("m_src"))
                lo(mlo(m), gates[:, 0, :], mhi[:, m, :], "m_hi", m + 1, "m_ready")
            for i in range(4):
                g = at_g("out", i)
                split(g + 1)
                for c in range(2):
                    m = 2 * i + c
                    dve.wait_ge(sem["out_mm"], due("out_mm", m + 1))
                    dve.wait_ge(sem["x_scaled"], due("x_scaled", m + 1))
                    residual(m, TILES.index((g, c)), G1, "out_out")
                    if m:
                        sum2(m - 1, m)
            sum2(KD - 1, KD)
            for w in range(2):
                following = w == 0 or L + 1 < DEPTH
                if w and following:
                    dve.wait_ge(sem["b_next_in"], 16 * (L + 1))
                    dve.wait_ge(sem["ada_t"], 4 * ADA_STEPS * (L + 1))
                    for v in range(2):
                        modulation(v, mod[:, KD * v:KD * (v + 1), :].rearrange("p j g -> p (j g)"),
                                   small[:, 32 + KD * v:32 + KD * (v + 1)])
                    dve.wait_ge(sem["mod_done"], now("mod_done"))
                    lane.start(L + 1)
                    split(0)
                    lane.start(L)
                dve.wait_ge(sem["stat_mm"], due("stat_mm", w + 1))
                TS(small[:, 76:86], ax[:, 3, 0:2 * NB], 1 / D_MODEL, None, ALU.mult).then_inc(sem["dve_order"], raised("dve_order"))
                dve.wait_ge(sem["dve_order"], now("dve_order"))
                TT(small[:, 66:71], small[:, 76:81], small[:, 76:81], ALU.mult).then_inc(sem["dve_order"], raised("dve_order"))
                dve.wait_ge(sem["dve_order"], now("dve_order"))
                TT(small[:, 66:71], small[:, 81:86], small[:, 66:71], ALU.subtract).then_inc(sem["dve_order"], raised("dve_order"))
                dve.wait_ge(sem["dve_order"], now("dve_order"))
                TS(small[:, 66:71], small[:, 66:71], 0.0, LN_EPS, ALU.max, ALU.add).then_inc(sem["ln_var"], raised("ln_var"))
                dve.wait_ge(sem["ln_sqrt"], due("ln_sqrt", w + 1))
                V.reciprocal(small[:, 86:91], small[:, 71:76]).then_inc(sem["dve_order"], raised("dve_order"))
                dve.wait_ge(sem["dve_order"], now("dve_order"))
                for i in range(2 * NB):
                    if i == NB:
                        STT(small[:, 91:96], small[:, 76:81], -1.0, small[:, 86:91], ALU.mult, ALU.mult)\
                            .then_inc(sem["dve_order"], raised("dve_order"))
                        dve.wait_ge(sem["dve_order"], now("dve_order"))
                    TS(diag[:, i, :], ident[:, :], small[:, 86 + i:87 + i], None, ALU.mult)\
                        .then_inc(sem["diag_out"], raised("diag_out"))
                dve.wait_ge(sem["bc_mm"], due("bc_mm", 2 * w + 1))
                for i in range(KD + 3 * following):
                    if i < KD:
                        TT(x[:, i, CTX], x[:, i, CTX], ax[:, 2, 0:P], ALU.mult).then_inc(sem["dve_order"], raised("dve_order"))
                        TT(x[:, i, LAT], x[:, i, LAT], ax[:, 0, :], ALU.mult).then_inc(sem["ln_scaled"], raised("ln_scaled"))
                    if following and 2 <= i < KD + 2:
                        dve.wait_ge(sem["ln_x"], due("ln_x", KD * w + i - 1))
                        h_src(2 + w, i - 2, (SH2, SH1)[w], (SC2, SC1)[w])
                    if following and i >= 3:
                        h_lo(2 + w, i - 3)
                if w:
                    break
                for hf in range(2):
                    for j in range(FH):
                        jj = FH * hf + j
                        g = at_g("up", jj)
                        split(g + 1)
                        sl = jj % 2
                        dve.wait_ge(sem["up_acc"], due("up_acc", jj + 1))
                        taps([gz[:, sl, :]], [ga[:, sl, :]], [lambda tp: parc("ff_w", 3 * jj + tp)], "up_taps")
                        dve.wait_ge(sem["up_gelu"], due("up_gelu", jj + 1))
                        dve.wait_ge(sem["up_mm"], due("up_mm", 2 * jj + 2))
                        TT(two(ga[:, sl, :]), two(ga[:, sl, :]), pair(TILES.index((g, 1))), ALU.mult).then_inc(sem["up_out"], raised("up_out"))
                        lo(actl[:, j, :], ga[:, sl, :], acth[:, j, :], "act_hi", jj + 1, "act_ready")
                        if L + 1 < DEPTH:
                            if jj == 0:
                                dve.wait_ge(sem["cond_rows"], L + 1)
                            ada_t(ADA_FFN[g])
                    for m in range(KD):
                        g = at_g("down", KD * hf + m)
                        if g + 1 < NG:
                            split(g + 1)
                        dve.wait_ge(sem["down_mm"], due("down_mm", KD * hf + m + 1))
                        dve.wait_ge(sem["x_scaled"], due("x_scaled", KD + m + 1))
                        residual(m, TILES.index((g, 0)), G2, "down_out")
                        if hf and m:
                            sum2(m - 1, KD + m)
                        if L + 1 < DEPTH and g in ADA_FFN:
                            ada_t(ADA_FFN[g])
                sum2(KD - 1, 2 * KD)
        lane.end()
        for b in range(NB):
            dve.wait_ge(sem["y_mm"], b + 1)
            V.tensor_copy(yout[:, b, 0:512], y_banks(b)[:, 0, :]).then_inc(sem["y_out"], 1)

    @block.gpsimd
    def _(pool):
        lane = Counts("pool_order")
        due, raised, now, slot_of = lane.due, lane.raised, lane.now, lane.slot_of
        G = nc.gpsimd
        G.memset(x[:, :, :], 0.0).then_inc(sem["x_zero"], 1)

        def zero_pads(bufs, event):
            n = 3 * len(bufs)
            for b in bufs:
                for a, e in ((0, 1), (C0 + SEQ, L0), (ROW - 1, ROW)):
                    n -= 1
                    G.memset(b[:, :, a:e], 0.0).then_inc(sem[event if n == 0 else "pool_order"], raised(event if n == 0 else "pool_order"))

        def scaled(h, first):
            for d in range(KD):
                pool.wait_ge(sem["h_ready"], due("h_ready", h * KD + d + 1))
                G.tensor_scalar(x[:, d, :], x[:, d, :], ALPHA, None, ALU.mult).then_inc(sem["x_scaled"], raised("x_scaled"))

        def shifted(w):
            pool.wait_ge(sem["ln_shift"], due("ln_shift", 2 * (w + 1)))
            for d in range(KD):
                pool.wait_ge(sem["ln_scaled"], due("ln_scaled", KD * w + d + 1))
                G.tensor_tensor(x[:, d, CTX], x[:, d, CTX], gz[:, 0, CTX], ALU.add).then_inc(sem["pool_order"], raised("pool_order"))
                G.tensor_tensor(x[:, d, LAT], x[:, d, LAT], gz[:, 0, LAT], ALU.add).then_inc(sem["ln_norm"], raised("ln_norm"))

        def sum1(event, first):
            for m in range(KD):
                pool.wait_ge(sem[event], due(event, first + m + 1))
                if m == 0:
                    G.tensor_copy(sums[:, 0, :], x[:, 0, :]).then_inc(sem["sum1_out"], raised("sum1_out"))
                else:
                    pool.wait_ge(sem["sum1_out"], now("sum1_out"))
                    G.tensor_tensor(sums[:, 0, :], sums[:, 0, :], x[:, m, :], ALU.add).then_inc(sem["sum1_out"], raised("sum1_out"))

        for L in range(DEPTH):
            lane.start(L)
            if L == 0:
                pool.wait_ge(sem["mlp_arg"], 3)
                zero_pads([hsrc], "pads_h")
            pool.wait_ge(sem["ln_x"], due("ln_x", 0))
            pool.dma_start(par[:, 0:NPAR], A["par"][L]).then_inc(sem["params_in"], 16)
            pool.wait_ge(sem["h_ready"], due("h_ready", KD))
            pool.dma_start(trig[:, :, :], A["trig"]).then_inc(sem["trig_in"], 16)
            pool.wait_ge(sem["qkv_out"], due("qkv_out", 4))
            zero_pads([f32(ath[:, :, :]), f32(atl[:, :, :])], "pads_at")
            pool.wait_ge(sem["vt_out"], due("vt_out", 4))
            pool.dma_start(A["out_k"][L], kout[:, :]).then_inc(sem["kv_dma"], 16)
            pool.dma_start(A["out_v"][L], vtok[:, 0, :]).then_inc(sem["kv_dma"], 16)
            pool.wait_ge(sem["kv_dma"], 32 * (L + 1))
            pool.dma_start(w3[:, :], A["w3"][L]).then_inc(sem["w3_in"], 16)
            pool.wait_ge(sem["xu_ready"], due("xu_ready", 4))
            pool.wait_ge(sem["z_out"], due("z_out", 12))
            for n, (a, b) in enumerate(((0, 4), (4, 6), (6, 8), (8, 10))):
                if n:
                    pool.wait_ge(sem["filt_out"], due("filt_out", 2 * n))
                pool.dma_start(filt[:, 2 + a % 4:2 + a % 4 + b - a, :], A["window"][:, a:b, :])\
                    .then_inc(sem["win_in"], 16)
                pool.wait_ge(sem["win_in"], 64 * L + 16 * (n + 1))
            pool.wait_ge(sem["y_ready"], due("y_ready", 10))
            pool.wait_ge(sem["pads_at"], now("pads_at"))
            zero_pads([hsrc], "pads_h")
            scaled(1, 0)
            pool.wait_ge(sem["m_ready"], due("m_ready", KD))
            pool.wait_ge(sem["x_scaled"], now("x_scaled"))
            zero_pads([hsrc], "pads_h")
            sum1("out_out", 0)
            shifted(0)
            if L + 1 < DEPTH:
                pool.wait_ge(sem["bc_mm"], due("bc_mm", 2))
                pool.dma_start(crow[:, :, :], A["cond_rows"]).then_inc(sem["cond_rows_in"], 16)
            scaled(2, KD)
            if L + 1 < DEPTH:
                zero_pads([hsrc], "pads_h")
                pool.dma_start(small[:, 32:32 + 2 * KD], A["par"][L + 1][:, PAR["b_ada"]:PAR["b_ada"] + 2 * KD])\
                    .then_inc(sem["b_next_in"], 16)
            sum1("down_out", KD)
            shifted(1)
        lane.end()

    st.close()


def _dft_constants():
    def forward(freqs, n_in, length):
        ang = 2 * np.pi * np.outer(np.arange(n_in), freqs) / length
        return np.cos(ang), -np.sin(ang)

    def back(freqs, n_out, length):
        ang = 2 * np.pi * np.outer(freqs, np.arange(n_out)) / length
        return 2 * np.cos(ang) / length, -2 * np.sin(ang) / length

    f0, i0, i1 = [], [], []
    N, NC = 2 * DEC_SEQ, 2 * SEQ
    kk = np.arange(SEQ // 2)
    zero = np.zeros((SEQ, SEQ // 2))
    ev, od = forward(2 * kk, SEQ, NC), forward(2 * kk + 1, SEQ, NC)
    ny = np.cos(np.pi * np.arange(SEQ))
    evi = ev[1].copy()
    evi[:, 0] = ny
    ctx = [np.hstack([ev[0], zero]), np.hstack([zero, od[0]]), np.hstack([evi, zero]), np.hstack([zero, od[1]])]
    br, bi = back(np.concatenate([2 * kk, 2 * kk + 1]), SEQ, NC)
    br[0] /= 2
    bi[0] = np.cos(np.pi * np.arange(SEQ)) / NC
    cinv = [br, bi]
    k4 = np.arange(P)
    lat = []
    for add in (0, 2):
        re, im = forward(4 * k4 + add, DEC_SEQ // 2, N)
        if add == 0:
            im = im.copy()
            im[:, 0] = np.cos(np.pi * np.arange(DEC_SEQ // 2))
        lat += [re[:P], re[P:], im[:P], im[P:]]
        br, bi = back(4 * k4 + add, DEC_SEQ, N)
        if add == 0:
            br[0] /= 2
            bi[0] = np.cos(np.pi * np.arange(DEC_SEQ)) / N
        i0 += [br, bi]
    f0 = ctx + lat + cinv
    f1 = []
    for o in range(2):
        fr = 2 * (P * o + np.arange(P)) + 1
        re, im = forward(fr, DEC_SEQ, N)
        f1 += [m[P * b:P * (b + 1)] for m in (re, im) for b in range(4)]
        i1 += list(back(fr, DEC_SEQ, N))
    cat = lambda xs: np.ascontiguousarray(np.hstack(xs).astype(np.float32))
    return {"F0": cat(f0), "F1": cat(f1), "I0": cat(i0), "I1": cat(i1)}


def _shape_constants():
    out = _dft_constants()
    out["ident"] = np.eye(P, dtype=np.float32)
    out["ones"] = np.ones((P, P), np.float32)
    r = np.zeros((P, P), np.float32)
    for a in range(0, P, 32):
        for i in range(16):
            r[a + 16 + i, a + i] = -1.0
            r[a + i, a + 16 + i] = 1.0
    out["rot"] = r
    inv = 1.0 / (10000.0 ** (np.arange(0, 32, 2, dtype=np.float32) / np.float32(32)))
    pos = np.stack([np.repeat(np.arange(DEC_SEQ // 64), 64), np.tile(np.arange(64), DEC_SEQ // 64)])
    ang = pos.astype(np.float32)[:, None, :] * inv.astype(np.float32)[None, :, None]
    ang = np.tile(np.concatenate([ang, ang], axis=1).reshape(HD, DEC_SEQ), (2, 1))
    out["trig"] = np.ascontiguousarray(np.stack([np.cos(ang), np.sin(ang)], axis=1).astype(np.float32))
    i, j = np.indices((P, P))
    zero = np.zeros((P, P))
    prev, nxt = np.where(j >= i, 0, -1e30), np.where(j <= i, 0, -1e30)
    out["mask"] = np.hstack([zero, prev, zero, nxt, zero]).astype(np.float32)

    def times(L):
        t = np.linspace(0.0, 1.0, L, dtype=np.float32)
        w = (2.0 * math.pi * np.arange(L, dtype=np.float32) / L).astype(np.float32)
        f = np.linspace(1e-4, 15, 16, dtype=np.float32)
        z = w[:, None] * f[None, :]
        feats = np.concatenate([t[:, None], np.cos(z), -np.sin(z)], axis=1).astype(np.float32)
        rates = np.abs(np.linspace(math.log(1e-2) / 1.5, math.log(1e-2) / 0.3, HY_W, dtype=np.float32))
        window = np.exp(-t[:, None] * rates[None, :]).astype(np.float32)
        back = (L - np.arange(L)) % L
        wback = window[back].copy()
        wback[0] = 0.0
        return feats, feats[back], window, wback

    fc, fcb, wc, wcb = times(SEQ)
    fl, flb, wl, wlb = times(DEC_SEQ)
    out["feat"] = np.ascontiguousarray(np.concatenate([fc, fcb, fl, flb]).T)
    blocks = [wc, wcb]
    for b in range(4):
        blocks += [wl[P * b:P * (b + 1)], wlb[P * b:P * (b + 1)]]
    out["window"] = np.ascontiguousarray(np.stack(blocks, axis=1))
    return out


def _layouts(i):
    out = {}
    D = DEPTH

    def chunks(w, tiles):
        d, kk, n = w.shape
        w = w.reshape(d, kk // P, P, n // (P * tiles), tiles, P)
        return np.ascontiguousarray(w.transpose(0, 3, 2, 4, 1, 5)).reshape(d, n // (P * tiles), P, -1)

    w_in = np.asarray(i["w_in"])
    qw, rest = w_in[..., :512], w_in[..., 512:]
    heads = [g * 4 + j for j in range(4) for g in range(2)]
    qw = qw.reshape(D, D_MODEL, NH, HD)[:, :, heads].reshape(D, D_MODEL, 512)
    out["w_q"] = chunks(qw, 2)
    out["w_k"], out["w_v"] = chunks(rest[..., 0:P], 1), chunks(rest[..., P:2 * P], 1)
    z = rest[..., 2 * P:2 * P + 3 * HY_W].reshape(D, D_MODEL, 12, P)
    order = [t for n in range(4) for t in (4 + n, 8 + n)] + [0, 1, 2, 3]
    out["w_z"] = chunks(z[:, :, order].reshape(D, D_MODEL, 12 * P), 2)
    ga = rest[..., 2 * P + 3 * HY_W:].reshape(D, D_MODEL, 2, KD, P)
    out["w_gate"] = chunks(ga.transpose(0, 1, 3, 2, 4).reshape(D, D_MODEL, 16 * P), 2)
    pa = np.asarray(i["w_pa"]).reshape(D, NH, HD, D_MODEL)[:, heads].reshape(D, 512, D_MODEL)
    out["w_proj"] = chunks(np.concatenate([pa, np.asarray(i["w_pb"])], axis=1), 1)
    out["w_out"] = chunks(np.asarray(i["w_out"]), 2)
    up = np.asarray(i["w_up"]).reshape(D, D_MODEL, 2, NFF, P).transpose(0, 1, 3, 2, 4)
    out["w_up"] = chunks(up.reshape(D, D_MODEL, 2 * D_FF), 2)
    down = np.asarray(i["w_down"]).reshape(D, 2, D_FF // 2, D_MODEL)
    out["w_down"] = np.ascontiguousarray(np.concatenate([chunks(down[:, 0], 1), chunks(down[:, 1], 1)], axis=1))
    w_ada = np.asarray(i["w_ada"])
    out["ada"] = chunks(w_ada, 2)[0]
    w_t = w_ada[1:].transpose(0, 2, 1).reshape(D - 1, ADA_STEPS, 2, P, D_MODEL)
    out["ada_t"] = np.ascontiguousarray(w_t.transpose(0, 1, 3, 2, 4)).reshape(D - 1, ADA_STEPS, P, CHUNK)
    col = lambda v: np.asarray(v).reshape(D, -1, P).transpose(0, 2, 1)
    tap = lambda w: np.asarray(w).reshape(D, 3, -1, P).transpose(0, 3, 2, 1).reshape(D, P, -1)
    sink = np.broadcast_to(np.asarray(i["attn_sink"])[:, None, heads], (D, P, NH))
    ck = np.asarray(i["cache_k"])[0].reshape(D, PAST, P)
    cv = np.asarray(i["cache_v"])[0].reshape(D, PAST, P)
    out["par"] = np.ascontiguousarray(np.concatenate([
        col(i["b_ada"]), tap(i["hy_conv_w"]), col(i["hy_conv_b"]), col(i["hy_bias"]), col(i["ln1_g"]),
        col(i["ln1_b"]), col(i["ln2_g"]), col(i["ln2_b"]), tap(i["ffn_conv_w"]), col(i["ffn_conv_b"]),
        sink, ck, cv], axis=2))
    c2 = np.stack([np.asarray(i["c_ctx"]), np.asarray(i["c"])[0]], axis=-1)
    out["cond_rows"] = np.ascontiguousarray(np.broadcast_to(c2.T, (P, 2, D_MODEL)))
    out["cond"] = np.ascontiguousarray(c2.reshape(KD, P, 2).transpose(1, 0, 2))
    hid = np.asarray(i["filt_w2"]).shape[1]
    out["w1"] = np.ascontiguousarray(np.concatenate(list(np.asarray(i["filt_w1"])), axis=1))
    w2 = np.zeros((P, P), np.float32)
    w3 = np.zeros((D, P, 2 * HY_W), np.float32)
    for l in range(D):
        w2[hid * l:hid * (l + 1), hid * l:hid * (l + 1)] = np.asarray(i["filt_w2"])[l]
        w3[l, hid * l:hid * (l + 1)] = np.asarray(i["filt_w3"])[l]
    out["w2"], out["w3"] = w2, w3
    out["mlpv"] = np.ascontiguousarray(np.stack(
        [np.asarray(i[n]).reshape(-1) for n in ("filt_b1", "filt_freq1", "filt_b2", "filt_freq2")], axis=1))
    out["x_prompt"], out["x_sample"] = np.asarray(i["x_prompt"]), np.asarray(i["x_sample"])
    return out


def kernel(**inputs):
    import concourse.bacc as bacc
    from concourse.bass_utils import run_bass_kernel_spmd

    nc = bacc.Bacc("TRN2", target_bir_lowering=False, num_devices=1)
    arrays = {**_layouts(inputs), **_shape_constants()}
    A = {n: nc.dram_tensor("in_" + n, a.shape, mybir.dt.from_np(a.dtype), kind="ExternalInput").ap()
         for n, a in arrays.items()}
    outs = {"y_prompt": (1, SEQ, D_MODEL), "y_sample": (1, DEC_SEQ, D_MODEL),
            "out_k": (DEPTH, SEQ, NKV * HD), "out_v": (DEPTH, SEQ, NKV * HD)}
    for n, s in outs.items():
        A[n] = nc.dram_tensor("res_" + n, s, F32, kind="ExternalOutput").ap()
    _program(nc, A)
    r = run_bass_kernel_spmd(nc, [{"in_" + n: a for n, a in arrays.items()}], core_ids=[0]).results[0]
    cache = (1, DEPTH, SEQ, NKV, HD)
    return (r["res_y_prompt"], r["res_y_sample"], r["res_out_k"].reshape(cache), r["res_out_v"].reshape(cache))
```
